# Optimizing a Trainium2 kernel written in Bass

```python
import jax, jax.numpy as jnp
from jax import lax
import numpy as np

D_MODEL = 1024
BATCH = 1
SEQ = 256
DEPTH = 2

CHUNK = 64
N_MIXERS = 2
N_SB_LAYERS = (DEPTH + 1) // 2
N_RG_LAYERS = DEPTH // 2

SB_HEADS = 16
SB_HEAD_DIM = D_MODEL // SB_HEADS
Q_BLOCK = 128

RG_WIDTH = D_MODEL
RG_BLOCKS = 16
RG_BLOCK_DIM = RG_WIDTH // RG_BLOCKS
RG_CONV = 4
RG_C = 8.0

D_FF = 4 * D_MODEL
EPS = 1e-6


def rms_norm(x, g):
    xf = x.astype(jnp.float32)
    y = xf * lax.rsqrt(jnp.mean(xf * xf, axis=-1, keepdims=True) + EPS)
    return (y * g.astype(jnp.float32)).astype(x.dtype)

def stick_breaking_attention(h, w_qkv, w_o):
    B, S, _ = h.shape
    qkv = (h @ w_qkv).reshape(B, S, 3, SB_HEADS, SB_HEAD_DIM)
    q = qkv[:, :, 0].transpose(0, 2, 1, 3)
    k = qkv[:, :, 1].transpose(0, 2, 1, 3)
    v = qkv[:, :, 2].transpose(0, 2, 1, 3)
    scale = SB_HEAD_DIM ** -0.5
    outs = []
    for start in range(0, S, Q_BLOCK):
        end = start + Q_BLOCK
        qb = q[:, :, start:end]
        kb = k[:, :, :end]
        vb = v[:, :, :end]
        z = jnp.einsum('bhqd,bhkd->bhqk', qb, kb).astype(jnp.float32) * scale
        q_pos = start + jnp.arange(Q_BLOCK)[:, None]
        k_pos = jnp.arange(end)[None, :]
        mask = k_pos < q_pos
        log_keep = jnp.where(mask, jax.nn.log_sigmoid(-z), 0.0)
        after = lax.cumsum(log_keep, axis=3, reverse=True) - log_keep
        w = jnp.where(mask, jnp.exp(jax.nn.log_sigmoid(z) + after), 0.0)
        outs.append(jnp.einsum('bhqk,bhkd->bhqd', w.astype(vb.dtype), vb))
    o = jnp.concatenate(outs, axis=2).transpose(0, 2, 1, 3).reshape(B, S, D_MODEL)
    return o @ w_o

def causal_depthwise_conv(x, w, b):
    S = x.shape[1]
    xp = jnp.pad(x, ((0, 0), (RG_CONV - 1, 0), (0, 0)))
    y = b
    for tap in range(RG_CONV):
        y = y + xp[:, tap:tap + S] * w[tap]
    return y

def lru_combine(e1, e2):
    a1, b1 = e1
    a2, b2 = e2
    return a1 * a2, a2 * b1 + b2

def rglru_block(h, w_in, conv_w, conv_b, w_a, b_a, w_x, b_x, lam, w_o):
    B, S, _ = h.shape
    proj = h @ w_in
    gate = jax.nn.gelu(proj[..., :RG_WIDTH])
    xc = causal_depthwise_conv(proj[..., RG_WIDTH:], conv_w, conv_b)
    xh = xc.reshape(B, S, RG_BLOCKS, RG_BLOCK_DIM)
    r = jax.nn.sigmoid(jnp.einsum('bshi,hij->bshj', xh, w_a).reshape(B, S, RG_WIDTH) + b_a)
    i = jax.nn.sigmoid(jnp.einsum('bshi,hij->bshj', xh, w_x).reshape(B, S, RG_WIDTH) + b_x)
    log_a = (-RG_C * r.astype(jnp.float32)) * jax.nn.softplus(-lam.astype(jnp.float32))
    a = jnp.exp(log_a)
    mult = jnp.sqrt(-jnp.expm1(2.0 * log_a))
    bterm = mult * (i * xc).astype(jnp.float32)
    _, hs = lax.associative_scan(lru_combine, (a, bterm), axis=1)
    y = hs.astype(h.dtype) * gate
    return y @ w_o

def squared_relu_mlp(h, w1, w2):
    u = jax.nn.relu(h @ w1)
    return (u * u) @ w2

def first_inputs(seed: int = 0) -> dict:
    key = jax.random.key(seed)
    ks = jax.random.split(key, 20)
    f32 = jnp.float32
    res_scale = (2.0 * DEPTH) ** -0.5
    x = jax.random.normal(ks[0], (BATCH, SEQ, D_MODEL), f32)
    norm_mix = 1.0 + 0.02 * jax.random.normal(ks[1], (DEPTH, D_MODEL), f32)
    norm_mlp = 1.0 + 0.02 * jax.random.normal(ks[2], (DEPTH, D_MODEL), f32)
    mlp_w1 = jax.random.normal(ks[3], (DEPTH, D_MODEL, D_FF), f32) * D_MODEL ** -0.5
    mlp_w2 = jax.random.normal(ks[4], (DEPTH, D_FF, D_MODEL), f32) * (D_FF ** -0.5 * res_scale)
    sb_w_qkv = jax.random.normal(ks[5], (N_SB_LAYERS, D_MODEL, 3 * D_MODEL), f32) * D_MODEL ** -0.5
    sb_w_o = jax.random.normal(ks[6], (N_SB_LAYERS, D_MODEL, D_MODEL), f32) * (D_MODEL ** -0.5 * res_scale)
    rg_w_in = jax.random.normal(ks[7], (N_RG_LAYERS, D_MODEL, 2 * RG_WIDTH), f32) * D_MODEL ** -0.5
    rg_conv_w = jax.random.normal(ks[8], (N_RG_LAYERS, RG_CONV, RG_WIDTH), f32) * RG_CONV ** -0.5
    rg_conv_b = 0.01 * jax.random.normal(ks[9], (N_RG_LAYERS, RG_WIDTH), f32)
    rg_w_a = jax.random.normal(ks[10], (N_RG_LAYERS, RG_BLOCKS, RG_BLOCK_DIM, RG_BLOCK_DIM), f32) * RG_BLOCK_DIM ** -0.5
    rg_b_a = 0.01 * jax.random.normal(ks[11], (N_RG_LAYERS, RG_WIDTH), f32)
    rg_w_x = jax.random.normal(ks[12], (N_RG_LAYERS, RG_BLOCKS, RG_BLOCK_DIM, RG_BLOCK_DIM), f32) * RG_BLOCK_DIM ** -0.5
    rg_b_x = 0.01 * jax.random.normal(ks[13], (N_RG_LAYERS, RG_WIDTH), f32)
    u = jax.random.uniform(ks[14], (N_RG_LAYERS, RG_WIDTH), f32, 0.9, 0.999)
    s = u ** (1.0 / RG_C)
    rg_lambda = jnp.log(s) - jnp.log1p(-s)
    rg_w_o = jax.random.normal(ks[15], (N_RG_LAYERS, RG_WIDTH, D_MODEL), f32) * (RG_WIDTH ** -0.5 * res_scale)
    norm_final = 1.0 + 0.02 * jax.random.normal(ks[16], (D_MODEL,), f32)
    return {'x': x, 'norm_mix': norm_mix, 'norm_mlp': norm_mlp, 'mlp_w1': mlp_w1, 'mlp_w2': mlp_w2,
            'sb_w_qkv': sb_w_qkv, 'sb_w_o': sb_w_o, 'rg_w_in': rg_w_in, 'rg_conv_w': rg_conv_w,
            'rg_conv_b': rg_conv_b, 'rg_w_a': rg_w_a, 'rg_b_a': rg_b_a, 'rg_w_x': rg_w_x,
            'rg_b_x': rg_b_x, 'rg_lambda': rg_lambda, 'rg_w_o': rg_w_o, 'norm_final': norm_final}

def first_block(x, norm_mix, norm_mlp, mlp_w1, mlp_w2, sb_w_qkv, sb_w_o, rg_w_in, rg_conv_w,
              rg_conv_b, rg_w_a, rg_b_a, rg_w_x, rg_b_x, rg_lambda, rg_w_o, norm_final):
    ia = 0
    ib = 0
    for layer in range(DEPTH):
        h = rms_norm(x, norm_mix[layer])
        if layer % N_MIXERS == 0:
            y = stick_breaking_attention(h, sb_w_qkv[ia], sb_w_o[ia])
            ia += 1
        else:
            y = rglru_block(h, rg_w_in[ib], rg_conv_w[ib], rg_conv_b[ib], rg_w_a[ib], rg_b_a[ib],
                            rg_w_x[ib], rg_b_x[ib], rg_lambda[ib], rg_w_o[ib])
            ib += 1
        x = x + y
        h = rms_norm(x, norm_mlp[layer])
        x = x + squared_relu_mlp(h, mlp_w1[layer], mlp_w2[layer])
    return rms_norm(x, norm_final)


DEPTH_2 = 1

N_META = 16
CONV_CH = 512
CONV_KERNEL = 31
RWKV_WIDTH = 512
RWKV_HEAD = 64
RWKV_HEADS = RWKV_WIDTH // RWKV_HEAD
RANK_W = 64
RANK_A = 64
RANK_G = 128
N_BRANCH = 2
SHIFT_TOTAL = 3 * RWKV_WIDTH + RANK_W + RANK_A + RANK_G
IN_SPLITS = [CONV_CH, 2 * CONV_CH, 2 * CONV_CH + SHIFT_TOTAL]
IN_TOTAL = 2 * CONV_CH + SHIFT_TOTAL + N_BRANCH * D_MODEL
RWKV_SPLITS = [RWKV_WIDTH, 2 * RWKV_WIDTH, 3 * RWKV_WIDTH, 3 * RWKV_WIDTH + RANK_W, 3 * RWKV_WIDTH + RANK_W + RANK_A]
PEER_HEADS = 8
PEER_NKEYS = 128
PEER_EXPERTS = PEER_NKEYS * PEER_NKEYS
PEER_DHALF = 128
PEER_TOPK = 16
TOK_BLOCK = 256
RMS_EPS = 1e-6
LN_EPS = 1e-5
GN_EPS = 64e-5


def rmsnorm(x, g):
    xf = x.astype(jnp.float32)
    y = xf * lax.rsqrt(jnp.mean(xf * xf, axis=-1, keepdims=True) + RMS_EPS)
    return (y * g.astype(jnp.float32)).astype(x.dtype)

def token_shift(z):
    return jnp.pad(z[:, :-1], ((0, 0), (1, 0), (0, 0)))

def conformer_conv(val, gate, conv_w, conv_b, ln_g, ln_b, w_out):
    u = val * jax.nn.sigmoid(gate)
    y = lax.conv_general_dilated(
        u, conv_w[:, None, :].astype(u.dtype), window_strides=(1,),
        padding=[(CONV_KERNEL - 1, 0)], dimension_numbers=('NWC', 'WIO', 'NWC'),
        feature_group_count=CONV_CH) + conv_b
    yf = y.astype(jnp.float32)
    mean = jnp.mean(yf, axis=-1, keepdims=True)
    var = jnp.mean(jnp.square(yf - mean), axis=-1, keepdims=True)
    yn = (yf - mean) * lax.rsqrt(var + LN_EPS) * ln_g + ln_b
    return jax.nn.silu(yn).astype(val.dtype) @ w_out

def wkv7_scan(r, decay, k, v, kk, a):
    def step(S, inp):
        r_t, w_t, k_t, v_t, kk_t, a_t = inp
        sa = jnp.einsum('bhvk,bhk->bhv', S, kk_t)
        S = (S * w_t[:, :, None, :]
             - sa[..., None] * (kk_t * a_t)[:, :, None, :]
             + v_t[..., None] * k_t[:, :, None, :])
        return S, jnp.einsum('bhvk,bhk->bhv', S, r_t)
    B, T, H, N = r.shape
    S0 = jnp.zeros((B, H, N, N), jnp.float32)
    xs = tuple(jnp.moveaxis(z, 1, 0) for z in (r, decay, k, v, kk, a))
    _, o = lax.scan(step, S0, xs)
    return jnp.moveaxis(o, 0, 1)

def rwkv7_mix(z, mu, w0, w_up, a0, a_up, g_up, k_k, k_a, r_k, gn_g, gn_b, w_out):
    B, T, _ = z.shape
    zf = z.astype(jnp.float32)
    zf = zf + (token_shift(zf) - zf) * mu
    r, k, v, lw, la, lg = jnp.split(zf, RWKV_SPLITS, axis=-1)
    w = -jax.nn.softplus(-(w0 + jnp.tanh(lw) @ w_up)) - 0.5
    decay = jnp.exp(-jnp.exp(w))
    a = jax.nn.sigmoid(a0 + la @ a_up)
    g = jax.nn.sigmoid(lg) @ g_up
    hd = lambda t: t.reshape(B, T, RWKV_HEADS, RWKV_HEAD)
    kk = hd(k * k_k)
    kk = kk * lax.rsqrt(jnp.maximum(jnp.sum(kk * kk, axis=-1, keepdims=True), 1e-24))
    k = k * (1.0 + (a - 1.0) * k_a)
    r_h, k_h, v_h, a_h = hd(r), hd(k), hd(v), hd(a)
    o = wkv7_scan(r_h, hd(decay), k_h, v_h, kk, a_h)
    mean = jnp.mean(o, axis=-1, keepdims=True)
    var = jnp.mean(jnp.square(o - mean), axis=-1, keepdims=True)
    o = ((o - mean) * lax.rsqrt(var + GN_EPS)).reshape(B, T, RWKV_WIDTH) * gn_g + gn_b
    bonus = jnp.sum(r_h * k_h * r_k, axis=-1, keepdims=True) * v_h
    o = (o + bonus.reshape(B, T, RWKV_WIDTH)) * g
    return o.astype(z.dtype) @ w_out

def peer_ffn(x, w_q, sub_keys, expert_u, expert_v):
    B, T, D = x.shape
    n_tok = B * T
    n_blocks = -(-n_tok // TOK_BLOCK)
    pad = n_blocks * TOK_BLOCK - n_tok
    xt = jnp.pad(x.reshape(n_tok, D), ((0, pad), (0, 0))).reshape(n_blocks, TOK_BLOCK, D)
    K = PEER_TOPK

    def block(xb):
        q = (xb @ w_q).reshape(TOK_BLOCK, PEER_HEADS, 2, PEER_DHALF)
        s = jnp.einsum('thcd,hcnd->thcn', q, sub_keys).astype(jnp.float32)
        top_s, top_i = lax.top_k(s, K)
        cand = top_s[:, :, 0, :, None] + top_s[:, :, 1, None, :]
        best_s, best_c = lax.top_k(cand.reshape(TOK_BLOCK, PEER_HEADS, K * K), K)
        i1 = jnp.take_along_axis(top_i[:, :, 0], best_c // K, axis=-1)
        i2 = jnp.take_along_axis(top_i[:, :, 1], best_c % K, axis=-1)
        e = (i1 * PEER_NKEYS + i2).reshape(TOK_BLOCK, PEER_HEADS * K)
        gate = jax.nn.softmax(best_s, axis=-1).reshape(TOK_BLOCK, PEER_HEADS * K)
        u = expert_u[e]
        act = jax.nn.gelu(jnp.einsum('td,ted->te', xb, u), approximate=False)
        coef = (gate * act.astype(jnp.float32)).astype(xb.dtype)
        return jnp.einsum('te,ted->td', coef, expert_v[e])

    y = lax.map(block, xt)
    return y.reshape(n_blocks * TOK_BLOCK, D)[:n_tok].reshape(B, T, D)

def second_inputs(seed: int = 0) -> dict:
    key = jax.random.key(seed)
    ks = jax.random.split(key, 32)
    f32 = jnp.float32
    L = DEPTH_2
    D = D_MODEL

    def nrm(k, shape, s):
        return jax.random.normal(k, shape, f32) * s

    return {
        "x": nrm(ks[0], (BATCH, SEQ, D), 1.0),
        "meta_tokens": nrm(ks[1], (N_META, D), 1.0),
        "g_mix": 1.0 + nrm(ks[2], (L, D), 0.01),
        "w_in": nrm(ks[3], (L, D, IN_TOTAL), D ** -0.5),
        "conv_w": nrm(ks[4], (L, CONV_KERNEL, CONV_CH), CONV_KERNEL ** -0.5),
        "conv_b": nrm(ks[5], (L, CONV_CH), 0.01),
        "conv_ln_g": 1.0 + nrm(ks[6], (L, CONV_CH), 0.01),
        "conv_ln_b": nrm(ks[7], (L, CONV_CH), 0.01),
        "w_conv_out": nrm(ks[8], (L, CONV_CH, D), CONV_CH ** -0.5),
        "mu_shift": jax.random.uniform(ks[9], (L, SHIFT_TOTAL), f32),
        "w0": jax.random.uniform(ks[10], (L, RWKV_WIDTH), f32, -6.0, -1.0),
        "w_up": nrm(ks[11], (L, RANK_W, RWKV_WIDTH), 0.1 * RANK_W ** -0.5),
        "a0": nrm(ks[12], (L, RWKV_WIDTH), 0.1),
        "a_up": nrm(ks[13], (L, RANK_A, RWKV_WIDTH), 0.1 * RANK_A ** -0.5),
        "g_up": nrm(ks[14], (L, RANK_G, RWKV_WIDTH), RANK_G ** -0.5),
        "k_k": 0.85 + nrm(ks[15], (L, RWKV_WIDTH), 0.02),
        "k_a": 1.0 + nrm(ks[16], (L, RWKV_WIDTH), 0.02),
        "r_k": nrm(ks[17], (L, RWKV_HEADS, RWKV_HEAD), 0.1),
        "gn_g": 1.0 + nrm(ks[18], (L, RWKV_WIDTH), 0.01),
        "gn_b": nrm(ks[19], (L, RWKV_WIDTH), 0.01),
        "w_rwkv_out": nrm(ks[20], (L, RWKV_WIDTH, D), RWKV_WIDTH ** -0.5),
        "w_o": nrm(ks[21], (L, D, D), D ** -0.5),
        "g_ffn": 1.0 + nrm(ks[22], (L, D), 0.01),
        "w_q": nrm(ks[23], (L, D, PEER_HEADS * 2 * PEER_DHALF), D ** -0.5),
        "sub_keys": nrm(ks[24], (L, PEER_HEADS, 2, PEER_NKEYS, PEER_DHALF), PEER_DHALF ** -0.5),
        "expert_u": nrm(ks[25], (L, PEER_EXPERTS, D), D ** -0.5),
        "expert_v": nrm(ks[26], (L, PEER_EXPERTS, D), PEER_HEADS ** -0.5),
        "g_final": 1.0 + nrm(ks[27], (D,), 0.01),
    }

def second_block(x, meta_tokens, g_mix, w_in, conv_w, conv_b, conv_ln_g, conv_ln_b, w_conv_out,
              mu_shift, w0, w_up, a0, a_up, g_up, k_k, k_a, r_k, gn_g, gn_b, w_rwkv_out,
              w_o, g_ffn, w_q, sub_keys, expert_u, expert_v, g_final):
    B = x.shape[0]
    meta = jnp.broadcast_to(meta_tokens[None].astype(x.dtype), (B, N_META, D_MODEL))
    h = jnp.concatenate([meta, x], axis=1)
    for l in range(DEPTH_2):
        z = rmsnorm(h, g_mix[l]) @ w_in[l]
        conv_val, conv_gate, rwkv_in, gate_logits = jnp.split(z, IN_SPLITS, axis=-1)
        y_a = conformer_conv(conv_val, conv_gate, conv_w[l], conv_b[l], conv_ln_g[l], conv_ln_b[l], w_conv_out[l])
        y_b = rwkv7_mix(rwkv_in, mu_shift[l], w0[l], w_up[l], a0[l], a_up[l], g_up[l],
                        k_k[l], k_a[l], r_k[l], gn_g[l], gn_b[l], w_rwkv_out[l])
        gate_a, gate_b = jnp.split(jax.nn.sigmoid(gate_logits), N_BRANCH, axis=-1)
        h = h + (gate_a * y_a + gate_b * y_b) @ w_o[l]
        h = h + peer_ffn(rmsnorm(h, g_ffn[l]), w_q[l], sub_keys[l], expert_u[l], expert_v[l])
    return rmsnorm(h, g_final)[:, N_META:]


def setup_inputs(seed=0):
    out = dict(first_inputs(seed))
    for name, value in second_inputs(seed + 1).items():
        if name != "x":
            out[name + "_2"] = value
    return out


def reference(
    x, norm_mix, norm_mlp, mlp_w1, mlp_w2, sb_w_qkv, sb_w_o, rg_w_in, rg_conv_w, rg_conv_b,
    rg_w_a, rg_b_a, rg_w_x, rg_b_x, rg_lambda, rg_w_o, norm_final, meta_tokens_2, g_mix_2,
    w_in_2, conv_w_2, conv_b_2, conv_ln_g_2, conv_ln_b_2, w_conv_out_2, mu_shift_2, w0_2,
    w_up_2, a0_2, a_up_2, g_up_2, k_k_2, k_a_2, r_k_2, gn_g_2, gn_b_2, w_rwkv_out_2, w_o_2,
    g_ffn_2, w_q_2, sub_keys_2, expert_u_2, expert_v_2, g_final_2,
):
    x = first_block(
        x, norm_mix, norm_mlp, mlp_w1, mlp_w2, sb_w_qkv, sb_w_o, rg_w_in, rg_conv_w, rg_conv_b,
        rg_w_a, rg_b_a, rg_w_x, rg_b_x, rg_lambda, rg_w_o, norm_final,
    )
    return second_block(
        x, meta_tokens_2, g_mix_2, w_in_2, conv_w_2, conv_b_2, conv_ln_g_2, conv_ln_b_2,
        w_conv_out_2, mu_shift_2, w0_2, w_up_2, a0_2, a_up_2, g_up_2, k_k_2, k_a_2, r_k_2,
        gn_g_2, gn_b_2, w_rwkv_out_2, w_o_2, g_ffn_2, w_q_2, sub_keys_2, expert_u_2, expert_v_2,
        g_final_2,
    )


_drawn_inputs = setup_inputs


def setup_inputs(seed=0):
    import zlib

    import numpy as np

    out = dict(_drawn_inputs(seed))
    spreads = {}
    factors = {'rg_conv_b': 2.675,
     'rg_b_a': 53.542,
     'rg_b_x': 25.585,
     'g_mix_2': 3.629,
     'conv_b_2': 28.884,
     'conv_ln_g_2': 40.568,
     'conv_ln_b_2': 43.136,
     'w_up_2': 6.665,
     'k_k_2': 18.789,
     'k_a_2': 3.194,
     'gn_g_2': 49.368,
     'gn_b_2': 47.184,
     'g_ffn_2': 25.792,
     'g_final_2': 31.603}
    for name, (base, spread) in spreads.items():
        noise = np.random.default_rng([zlib.crc32(name.encode()), seed]).standard_normal(out[name].shape)
        drawn = base * np.exp(spread * noise) if base else spread * noise
        out[name] = __import__('jax').numpy.asarray(drawn.astype(out[name].dtype))
    for name, factor in factors.items():
        out[name] = (out[name] * factor).astype(out[name].dtype)
    return out
```

```python
import math
import concourse.bass as bass
from concourse import mybir
from contextlib import ExitStack

F32 = mybir.dt.float32
F32R = mybir.dt.float32r
U32 = mybir.dt.uint32
ALU = mybir.AluOpType
ACT = mybir.ActivationFunctionType
AX = mybir.AxisListType

P = 128
D = 1024
KT = D // P
SEQ = 256
META = 16
TOK = META + SEQ
FF = 4 * D
HEADS = 16
HD = 64
CONV = 4
CK = 31
RW = 512
RT = RW // P
RH = RW // HD
CH = 64
NCH = 5
WT = NCH * CH
PADC = CH - META
ZT = 14
PH = 8
NK = 128
TOPK = 16
SEL = PH * TOPK
EPS, LN_EPS, GN_EPS = 1e-6, 1e-5, 64e-5
DECAY = -math.exp(-0.5)
LEVELS = 6

RING = 4
SLOT = 2048
BANKS = 8
GR = 16
UNITS = 4
MLP_UNITS = 2 * 2 * FF // 256
NEG = -3.0e38
N_ROW_DMAS = 27


class Plan:

    def __init__(self):
        self.n, self.at, self.uses = 0, {}, [0] * BANKS

    def add(self, name, bank=None):
        b = self.n % BANKS if bank is None else bank
        self.n += 1
        self.at[name] = (self.n, b, self.uses[b])
        self.uses[b] += 1

    def loop(self, name, rounds, banks, more=0):
        self.at[name] = (self.n, list(banks), [self.uses[b] for b in banks])
        self.n += rounds * (len(banks) + more)
        for b in banks:
            self.uses[b] += rounds


def make_plan():
    plan = Plan()
    for kt in range(KT):
        plan.add(f"xT{kt}")
    plan.add("par")
    plan.add("ms0")
    for m in range(KT):
        plan.add(f"q{m}")
    for m in range(KT):
        plan.add(f"k{m}")
    for j in range(4):
        for tt in range(2):
            plan.add(f"v{j}_{tt}")
    for i in range(HEADS + 2):
        if i < HEADS:
            plan.add(f"z{i}", i % 3)
        if i >= 2 and i % 2 == 1:
            plan.add(f"o{(i - 2) // 2}", 4 + ((i - 2) // 2) % 2)
    for m in range(KT):
        plan.add(f"wo{m}")
    for layer in range(2):
        if layer == 1:
            plan.add("ms2")
            for m in range(2 * KT):
                plan.add(f"rg{m}")
            for m in range(KT):
                plan.add(f"ri{m}")
            for m in range(KT):
                plan.add(f"rgo{m}")
        plan.add(f"ms{1 + 2 * layer}")
        plan.loop(f"up{layer}", 4, range(BANKS))
        plan.loop(f"down{layer}", 4, (0, 1), more=6)
    plan.add("ms4")
    plan.add("ms5")
    for m in range(ZT):
        plan.add(f"zr{m}")
    for m in range(RT):
        plan.add(f"val{m}")
    for m in range(RT):
        plan.add(f"cg{m}")
    for m in range(RT):
        plan.add(f"kks{m}")
    for m in range(RT):
        plan.add(f"wp{m}")
    for m in range(RT):
        plan.add(f"ap{m}")
    for m in range(RT):
        plan.add(f"gp{m}")
    for m in range(RT):
        plan.add(f"bon{m}")
    for tt in range(3):
        for s in range(3):
            plan.add(f"nat{s}_{tt}")
    for tt in range(3):
        for s in range(5 if tt else 3):
            for par in range(2):
                plan.add(f"mat{s}_{par}_{tt}")
    for lv in range(1, LEVELS):
        for tt in range(3):
            plan.add(f"Y{lv}_{tt}")
        for tt in range(3):
            if lv < LEVELS - 1:
                plan.add(f"XY{lv}_{tt}")
            plan.add(f"YX{lv}_{tt}")
    for tt in range(3):
        plan.add(f"GV_{tt}")
    for c in range(NCH):
        if c:
            plan.add(f"SA0_{c}")
            plan.add(f"SA1_{c}")
        plan.add(f"U_{c}")
        plan.add(f"S_{c}")
        if c:
            plan.add(f"OA_{c}")
            plan.add(f"OB_{c}")
    for m in range(RT):
        plan.add(f"gm{m}")
    for m in range(RT):
        plan.add(f"gv{m}")
    for m in range(2 * KT):
        plan.add(f"gl{m}")
    plan.add("lm")
    plan.add("lv")
    for m in range(KT):
        plan.add(f"yb{m}")
    for m in range(KT):
        plan.add(f"ya{m}")
    for m in range(KT):
        plan.add(f"wo2{m}")
    plan.add("ms6")
    for m in range(4):
        plan.add(f"key{m}")
    for m in range(5):
        for j in range(4 * m, min(4 * m + 4, 2 * PH)):
            plan.add(f"pq{j}")
        if m:
            plan.add(f"sc0_{m - 1}")
    for tt in range(2):
        for m in range(4 if tt else 0):
            plan.add(f"sc1_{m}")
        for m in range(2):
            plan.add(f"xn{tt}_{m}")
        for m in range(2):
            plan.add(f"hn{tt}_{m}")
    return plan


SLOTS = {}
_at = 0
for _name, _count in (("qkv", 12), ("wo", 4), ("up0", 16), ("down0", 16), ("rg_in", 8), ("rg_o", 4),
                      ("up1", 16), ("down1", 16), ("w_rwkv", 7), ("w_conv", 4), ("w_gate", 8),
                      ("rwkv_out", 2), ("conv_out", 2), ("wo2", 4), ("keys", 1), ("w_q", 8)):
    SLOTS[_name] = _at
    _at += _count
N_SLOTS = _at

RS_AT = {0: 1, 1: 2, 2: 3, 3: 4, 4: 5, 5: 6, "gn": 7, "ln": 8, 6: 9}
H_AT = {0: 0, 1: 1, 2: 2, 3: 3, 5: 4, 6: 5}


def make_release(plan):
    rel = {}

    def of(phase, *last_groups):
        for j, name in enumerate(last_groups):
            rel[SLOTS[phase] + j] = (False, plan.at[name][0])

    of("qkv", "q1", "q3", "q5", "q7", "k1", "k3", "k5", "k7", "v0_1", "v1_1", "v2_1", "v3_1")
    of("wo", *[f"wo{m}" for m in (1, 3, 5, 7)])
    of("rg_in", *[f"rg{m}" for m in range(1, 2 * KT, 2)])
    of("rg_o", *[f"rgo{m}" for m in (1, 3, 5, 7)])
    of("w_rwkv", *[f"zr{m}" for m in range(1, ZT, 2)])
    of("w_conv", "val1", "val3", "cg1", "cg3")
    of("w_gate", *[f"gl{m}" for m in range(1, 2 * KT, 2)])
    of("rwkv_out", "yb3", "yb7")
    of("conv_out", "ya3", "ya7")
    of("wo2", *[f"wo2{m}" for m in (1, 3, 5, 7)])
    of("keys", "key3")
    of("w_q", *[f"pq{m}" for m in range(1, 2 * PH, 2)])
    for layer in range(2):
        for s in range(MLP_UNITS // 2):
            rel[SLOTS[f"up{layer}"] + s] = (True, layer * MLP_UNITS + 2 * (s + 1))
    return rel


def build(nc, x, norm_mix, norm_mlp, mlp_w1, mlp_w2, sb_w_qkv, sb_w_o, rg_w_in, rg_conv_w,
          rg_conv_b, rg_w_a, rg_b_a, rg_w_x, rg_b_x, rg_lambda, rg_w_o, norm_final, meta_tokens,
          g_mix, w_in, conv_w, conv_b, conv_ln_g, conv_ln_b, w_conv_out, mu_shift, w0, w_up, a0,
          a_up, g_up, k_k, k_a, r_k, gn_g, gn_b, w_rwkv_out, w_o2, g_ffn, w_q, sub_keys, expert_u,
          expert_v, g_final, out):
    ctx = ExitStack()
    with ctx:
        def sb(name, shape, dt=F32):
            return ctx.enter_context(nc.sbuf_tensor(name, shape, dt))

        def sem(name):
            return ctx.enter_context(nc.semaphore(name))

        plan = make_plan()
        release = make_release(plan)
        bank = [ctx.enter_context(nc.psum_tensor(f"bank{b}", [P, 512], F32)) for b in range(BANKS)]

        wring = sb("wring", [P, RING, SLOT])
        xT = sb("xT", [P, KT, TOK])
        hT = sb("hT", [P, KT, TOK])
        sq = sb("sq", [P, KT, TOK])
        rs = sb("rs", [P, WT])
        rtmp = sb("rtmp", [P, WT])
        par = sb("par", [P, 320])
        ident = sb("ident", [P, P])
        mean_d = sb("mean_d", [P, P])
        mean_c = sb("mean_c", [P, P])
        head_sum = sb("head_sum", [P, P])
        head_mean = sb("head_mean", [P, P])
        neg_tri = sb("neg_tri", [P, P])
        neg_one = sb("neg_one", [P, P])
        attn_mask = sb("attn_mask", [P, 3 * P])
        strict = sb("strict", [P, CH])
        lower = sb("lower", [P, CH])
        incl = sb("incl", [P, CH])
        nincl = sb("nincl", [P, CH])
        eye = sb("eye", [P, CH])
        lvl = sb("lvl", [P, 2 * LEVELS, CH])
        reset = sb("reset", [P, WT])
        updown = sb("updown", [P, RW])
        gup = sb("gup", [P, RW])
        lamc = sb("lamc", [P, 5, KT])
        omka = sb("omka", [P, RT])
        pend = sb("pend", [P, RT, NCH])
        with ExitStack() as overlay:
            def split(name, *shape):
                return [overlay.enter_context(nc.sbuf_tensor(f"{name}_{part}", [P, *shape], F32R))
                        for part in ("high", "low")]

            u_hl = split("u", FF // P, SEQ)
            x_hl = split("x", KT, SEQ)
            w_hl = split("w", UNITS, KT, P)
        SPLIT_END = 2 * SEQ * (FF // P + KT) + 2 * UNITS * KT * P
        ARENA = 30000
        arena = sb("arena", [P, ARENA])

        def area(at, *shape):
            size = math.prod(shape)
            assert at + size <= ARENA, (at, shape)
            flat = arena[:, at:at + size]
            if len(shape) == 1:
                return flat
            if len(shape) == 2:
                return flat.rearrange("p (a b) -> p a b", b=shape[1])
            return flat.rearrange("p (a b c) -> p a b c", b=shape[1], c=shape[2])

        xnat = area(0, 2, D)
        metanat = area(2048, D)
        rows = area(3072, 3, P)
        qT, kT, V, oT = area(4096, KT, SEQ), area(6144, KT, SEQ), area(8192, 2, D), area(10240, KT, SEQ)
        lnz, sp, wexp = area(12288, 2, 384), area(13056, 2, 384), area(13824, 2, 384)
        mtmp = area(15000, P)
        utmp = area(SPLIT_END, 4, SEQ)
        gate = area(8192, KT, SEQ)
        xraw = area(10240, KT, SEQ + CONV - 1)
        xc = area(12312, KT, SEQ)
        rS, iS, aS, tS, mS = (area(14360 + 2048 * j, KT, SEQ) for j in range(5))
        bd = area(24600, 2, KT, P)
        U = area(0, RT, CK - 1 + TOK)
        zf = area(1208, ZT, WT)
        rZ, kZ, vZ = zf[:, 0:RT, :], zf[:, RT:2 * RT, :], zf[:, 2 * RT:3 * RT, :]
        kk, aa = area(5688, RT, WT), area(6968, RT, WT)
        gg, bonus = area(8248, RT, SEQ), area(9272, RT, SEQ)
        zr = area(10296, ZT, TOK + 1)
        ld, LP, Pd, Pi, Kh, Bh = (area(14118 + 1280 * j, RT, WT) for j in range(6))
        val, cg = area(21798, RT, TOK), area(22886, RT, TOK)
        tlw, slg = area(23974, WT), area(24294, SEQ)
        Nm, NT, X, XT, Y, MT = (area(10296 + 1536 * j, 3, RH, CH) for j in range(6))
        nat = [area(21798 + 1536 * j, 3, RW) for j in range(3)]
        G1, G2, G3 = area(26406, 3, RH, CH), area(27942, 2, RH, CH), area(28966, 2, RH, CH)
        owk, Yc, Uc, ST = area(16440, RT, SEQ), area(17464, RH, CH), area(17976, RH, CH), area(18488, 2, RT, CH)
        GAB = area(10296, 2 * KT, SEQ)
        cy, ct = area(19512, RT, SEQ), area(20536, RT, SEQ)
        osq, orr = area(26406, RT, SEQ), area(27430, RT, SEQ)
        mix, mt2 = area(21798, KT, SEQ), area(23846, SEQ)
        keyT, pq = area(0, 2 * PH, NK), area(2048, 2 * PH, SEQ)
        hnat, fnat = area(6144, 2, D), area(8192, 2, D)
        sc, sc2 = area(10240, 2 * PH, NK), area(12288, 2 * PH, NK)
        cand, cand2 = area(14336, PH, TOPK * TOPK), area(16384, PH, TOPK * TOPK)
        oh = cand2.rearrange("p h n -> p (h n)").rearrange("p (s k) -> p s k", k=TOPK)
        topv, topf = area(18432, 2 * PH, TOPK), area(18688, 2 * PH, TOPK)
        bv, rowf, colf, i1f, i2f = (area(18944 + 128 * j, PH, TOPK) for j in range(5))
        psm = area(19608, PH)
        gsel, dots, coef = (area(19620 + 256 * j, 2, SEL) for j in range(3))
        dot16 = area(20388, GR)
        coef16 = area(20404, GR)
        fsq = area(20420, 4)
        gfin = area(12288, D)
        yacc = area(10240, D)
        junk = area(20424, D)
        g_arena = area(21800, GR // 2, D)
        io16 = sb("io16", [P, TOPK])
        topi = sb("topi", [P, 2 * PH, TOPK], U32)
        bi = sb("bi", [P, PH, TOPK], U32)
        bt, bt2 = sb("bt", [P, PH, TOPK], U32), sb("bt2", [P, PH, TOPK], U32)
        eidx = sb("eidx", [P, 2, SEL], U32)
        eix = [sb(f"eix{h}", [P, GR], U32) for h in range(2)]

        def grow(j):
            if j < 8:
                return wring[:, j // 2, (j % 2) * D:(j % 2 + 1) * D]
            return g_arena[:, j - 8, :]

        consts_built, pool_chain, act_chain, dve_chain = map(sem, (
            "consts_built", "pool_chain", "act_chain", "dve_chain"))
        x_loaded, rows_loaded, bd_loaded, updown_loaded, gfin_loaded = map(sem, (
            "x_loaded", "rows_loaded", "bd_loaded", "updown_loaded", "gfin_loaded"))
        w_loaded = [sem(f"w_loaded{j}") for j in range(RING)]
        group_done = sem("group_done")
        bank_free = [sem(f"bank_free{b}") for b in range(BANKS)]
        x_ready, sq_ready, mean_ready, rs_ready, h_ready = map(sem, (
            "x_ready", "sq_ready", "mean_ready", "rs_ready", "h_ready"))
        lnz_ready, sp_ready, cum_done, w_ready, o_done, u_step = map(sem, (
            "lnz_ready", "sp_ready", "cum_done", "w_ready", "o_done", "u_step"))
        xg_ready, x_high, w_high, w_split = map(sem, ("xg_ready", "x_high", "w_high", "w_split"))
        lam_ready, xc_ready, ri_ready, at_ready, m_ready, mroot_ready, y_ready = map(sem, (
            "lam_ready", "xc_ready", "ri_ready", "at_ready", "m_ready", "mroot_ready", "y_ready"))
        zf_ready, kks_ready, lw_ready, kkn_ready, ksq_ready, lp_ready, p_ready, rk_ready, kb_ready = map(sem, (
            "zf_ready", "kks_ready", "lw_ready", "kkn_ready", "ksq_ready", "lp_ready", "p_ready",
            "rk_ready", "kb_ready"))
        mt_ready, yc_ready, st_ready, owk_ready, osq_ready = map(sem, (
            "mt_ready", "yc_ready", "st_ready", "owk_ready", "osq_ready"))
        cy_ready, csq_ready, cin_ready, cin_sig, yb_in, mix_ready = map(sem, (
            "cy_ready", "csq_ready", "cin_ready", "cin_sig", "yb_in", "mix_ready"))
        io_ready, eidx_ready, gsel_ready, gsel_exp = map(sem, (
            "io_ready", "eidx_ready", "gsel_ready", "gsel_exp"))
        row_loaded = [sem(f"row_loaded{j}") for j in range(GR)]
        rows_free, eix_copied, slot_seen, dot_saved, coef_copied, dots_ready, gelu_ready = map(sem, (
            "rows_free", "eix_copied", "slot_seen", "dot_saved", "coef_copied", "dots_ready", "gelu_ready"))
        y_ready2, fsum_ready, fin_ready, out_written = map(sem, (
            "y_ready2", "fsum_ready", "fin_ready", "out_written"))

        def norm_cols(j):
            return slice(0, TOK) if j == 5 else slice(META, TOK)

        real = slice(META, TOK)
        block = ctx.enter_context(nc.Block())

        def wait_group(eng, name):
            n, b, _ = plan.at[name]
            eng.wait_ge(group_done, n)
            return bank[b]

        def free(name):
            return bank_free[plan.at[name][1]]

        def wait_out(eng, *names):
            for name in names:
                _, b, used = plan.at[name]
                eng.wait_ge(bank_free[b], used + 1)

        def raw_unit(j):
            w = wring[:, (j // 2) % RING, :].rearrange("p (k n) -> p k n", n=256)
            return w[:, :, (j % 2) * P:(j % 2 + 1) * P]

        @block.sync
        def _(sp_):
            def load(s, src, kt, cols):
                if s >= RING:
                    is_split, n = release[s - RING]
                    sp_.wait_ge(w_split if is_split else group_done, n)
                dst = wring[:, s % RING, 0:kt * cols].rearrange("p (k n) -> p k n", n=cols)
                sp_.dma_start(dst, src).then_inc(w_loaded[s % RING], 16)

            def load_columns(name, w, c0, count):
                for j in range(count):
                    load(SLOTS[name] + j,
                         w.rearrange("(k p) n -> p k n", p=P)[:, :, c0 + 256 * j:c0 + 256 * (j + 1)], KT, 256)

            def load_mlp(layer):
                s0, n0 = SLOTS[f"up{layer}"], layer * MLP_UNITS
                up = mlp_w1[layer].rearrange("(k p) (r n) -> p k r n", p=P, n=256)
                down = mlp_w2[layer].rearrange("(q k p) (r n) -> q p k r n", p=P, k=KT, n=256)
                for j in range(RING):
                    load(s0 + j, up[:, :, j, :], KT, 256)
                with sp_.Fori(0, 3, 1) as i:
                    for j in range(RING):
                        sp_.wait_ge(w_split, i * (2 * RING) + (n0 + 2 * (j + 1)))
                        sp_.dma_start(wring[:, (s0 + j) % RING, :].rearrange("p (k n) -> p k n", n=256),
                                      up[:, :, bass.ds(i * RING + (RING + j), 1), :].rearrange("p k r n -> p k (r n)")
                                      ).then_inc(w_loaded[(s0 + j) % RING], 16)
                with sp_.Fori(0, 4, 1) as i:
                    for j in range(RING):
                        sp_.wait_ge(w_split, i * (2 * RING) + (n0 + 3 * 2 * RING + 2 * (j + 1)))
                        sp_.dma_start(wring[:, (s0 + j) % RING, :].rearrange("p (k n) -> p k n", n=256),
                                      down[j][:, :, i, :]).then_inc(w_loaded[(s0 + j) % RING], 16)

            load_columns("qkv", sb_w_qkv[0], 0, 12)
            load_columns("wo", sb_w_o[0], 0, 4)
            load_mlp(0)
            for j in range(8):
                c0 = (D if j < 4 else 0) + 256 * (j % 4)
                load(SLOTS["rg_in"] + j, rg_w_in[0].rearrange("(k p) n -> p k n", p=P)[:, :, c0:c0 + 256], KT, 256)
            load_columns("rg_o", rg_w_o[0], 0, 4)
            load_mlp(1)
            load_columns("w_rwkv", w_in[0], 1024, 7)
            load_columns("w_conv", w_in[0], 0, 4)
            load_columns("w_gate", w_in[0], 1024 + 1792, 8)
            for name, w in (("rwkv_out", w_rwkv_out), ("conv_out", w_conv_out)):
                for j in range(2):
                    load(SLOTS[name] + j,
                         w[0].rearrange("(k p) n -> p k n", p=P)[:, :, 512 * j:512 * (j + 1)], RT, 512)
            load_columns("wo2", w_o2[0], 0, 4)
            load(SLOTS["keys"], sub_keys[0].rearrange("h c n d -> n (h c) d"), 2 * PH, NK)
            load_columns("w_q", w_q[0], 0, 8)
            for tt in range(2):
                sp_.wait_ge(fin_ready, tt + 1)
                sp_.dma_start(out[0, tt * P:(tt + 1) * P, :], yacc).then_inc(out_written, 16)
            sp_.wait_ge(out_written, 32)

        @block.gpsimd
        def _(pool):
            chain = [0]

            def link(ins):
                chain[0] += 1
                ins.then_inc(pool_chain, 1)
                pool.wait_ge(pool_chain, chain[0])

            g = nc.gpsimd

            def keep(t, pattern, base, mult, fill=0.0):
                link(g.affine_select(out=t, in_=t, compare_op=ALU.is_ge, fill=fill, base=base,
                                     pattern=pattern, channel_multiplier=mult))

            link(g.memset(ident[:], 0.0))
            link(g.affine_select(out=ident[:], in_=ident[:], compare_op=ALU.not_equal, fill=1.0, base=0,
                                 pattern=[[-1, P]], channel_multiplier=1))
            g.memset(mean_d[:], 1.0 / D).then_inc(consts_built, 1)
            link(g.memset(neg_one[:], -1.0))
            link(g.memset(neg_tri[:], -1.0))
            keep(neg_tri[:], [[-1, P]], 0, 1)
            link(g.memset(attn_mask[:], 1.0))
            for c in (0, 2):
                keep(attn_mask[:, c * P:(c + 1) * P], [[1, P]], -1, -1)
            link(g.memset(mean_c[:], 1.0 / RW))
            link(g.memset(head_sum[:], 1.0))
            hs = head_sum[:].rearrange("p (b j) -> p b j", j=HD)
            keep(hs, [[-HD, 2], [0, HD]], 0, 1)
            keep(hs, [[HD, 2], [0, HD]], HD - 1, -1)
            link(g.tensor_scalar(head_mean[:], head_sum[:], 1.0 / HD, None, ALU.mult))

            def diagonal(dst, make):
                make()
                link(g.tensor_copy(dst[0:CH], mtmp[0:CH, 0:CH]))
                link(g.tensor_copy(dst[CH:P], mtmp[CH:P, CH:P]))

            def tri(step, base, mult):
                def make():
                    link(g.memset(mtmp, 1.0))
                    keep(mtmp, [[step, P]], base, mult)
                return make

            diagonal(strict[:], tri(1, -1, -1))
            diagonal(lower[:], tri(-1, -1, 1))
            diagonal(incl[:], tri(1, 0, -1))
            link(g.tensor_scalar(nincl[:], incl[:], -1.0, None, ALU.mult))
            link(g.tensor_copy(eye[0:CH], ident[0:CH, 0:CH]))
            link(g.tensor_copy(eye[CH:P], ident[CH:P, CH:P]))
            for lv in range(LEVELS):
                b = 1 << lv
                nb = P // (2 * b)

                def block_ts():
                    link(g.memset(mtmp, 1.0))
                    m4 = mtmp.rearrange("p (m h j) -> p m h j", h=2, j=b)
                    keep(m4, [[-2 * b, nb], [-P, 2], [0, b]], -b, 1)
                    keep(m4, [[2 * b, nb], [0, 2], [0, b]], 2 * b - 1, -1)

                def block_st():
                    link(g.memset(mtmp, 1.0))
                    m4 = mtmp.rearrange("p (m h j) -> p m h j", h=2, j=b)
                    keep(m4, [[-2 * b, nb], [P, 2], [0, b]], -P, 1)
                    keep(m4, [[2 * b, nb], [0, 2], [0, b]], b - 1, -1)

                diagonal(lvl[:, lv, :], block_ts)
                diagonal(lvl[:, LEVELS + lv, :], block_st)
            link(g.memset(reset[:], 1.0))
            link(g.memset(reset[:].rearrange("p (c j) -> p c j", j=CH)[:, :, 0:1], 0.0))
            g.iota(io16[:], [[1, TOPK]], base=0, channel_multiplier=0,
                   allow_small_or_imprecise_dtypes=True).then_inc(io_ready, 1)
            pool.sem_inc(consts_built, 1)
            pool.dma_start(updown[0:64, :], w_up[0]).then_inc(updown_loaded, 16)
            pool.dma_start(updown[64:128, :], a_up[0]).then_inc(updown_loaded, 16)
            pool.dma_start(gup[:], g_up[0]).then_inc(updown_loaded, 16)

            def split_low(layer):
                n0 = layer * MLP_UNITS
                with pool.Fori(0, MLP_UNITS // 8, 1) as i:
                    for j in range(8):
                        pool.wait_ge(w_high, i * 8 + (n0 + j + 1))
                        g.tensor_tensor(w_hl[1][:, j % UNITS], raw_unit(j), w_hl[0][:, j % UNITS].bitcast(F32),
                                        ALU.subtract).then_inc(w_split, 1)

            split_low(0)
            pool.wait_ge(group_done, plan.at["ms2"][0])
            link(g.memset(bd, 0.0))
            for s_, w in ((0, rg_w_a), (1, rg_w_x)):
                wv = w[0].rearrange("(k two) i j -> two i k j", two=2)
                for half in range(2):
                    pool.dma_start(bd[half * HD:(half + 1) * HD, s_, :, half * HD:(half + 1) * HD],
                                   wv[half]).then_inc(bd_loaded, 16)
            split_low(1)
            for tt in range(2):
                for which, table in ((0, expert_u), (1, expert_v)):
                    first = (2 * tt + which) * (SEL // GR)
                    if which == 0:
                        pool.wait_ge(eidx_ready, tt + 1)
                    with pool.Fori(0, SEL // GR // 2, 1) as i:
                        for half in range(2):
                            r16 = i * (2 * GR) + (first + half) * GR
                            pool.wait_ge(rows_free, r16 + 1)
                            pool.sem_inc(slot_seen, 1)
                            g.tensor_copy(eix[half][:], eidx[:, tt, bass.ds(i * (2 * GR) + half * GR, GR)]
                                          ).then_inc(eix_copied, 1)
                            pool.wait_ge(eix_copied, i * 2 + (first + half + 1))
                            for j in range(GR):
                                pool.wait_ge(rows_free, r16 + (j + 1))
                                pool.sem_inc(slot_seen, 1)
                                g.indirect_dma_start(
                                    out=grow(j), out_offset=None, in_=table[0],
                                    in_offset=bass.IndirectOffsetOnAxis(ap=eix[half][:, j:j + 1], axis=0)
                                ).then_inc(row_loaded[j], 16)

        @block.scalar
        def _(act):
            chain = [0]
            a = nc.scalar

            def link(ins):
                chain[0] += 1
                ins.then_inc(act_chain, 1)
                act.wait_ge(act_chain, chain[0])

            act.dma_start(xnat, x[0].rearrange("(t p) n -> p t n", p=P)).then_inc(x_loaded, 16)
            act.dma_start(metanat[0:META, :], meta_tokens).then_inc(x_loaded, 16)

            def row(t, at, v, r):
                act.dma_start(rows[at:at + r, t, :], v.rearrange("(r p) -> r p", p=P)).then_inc(rows_loaded, 16)

            for v, src in enumerate((norm_mix[0], norm_mix[1], norm_mlp[0], norm_mlp[1], norm_final)):
                row(0, v * KT, src, KT)
            for v in range(CONV):
                row(0, (5 + v) * KT, rg_conv_w[0, v], KT)
            for v, src in enumerate((rg_conv_b[0], rg_b_a[0], rg_b_x[0], rg_lambda[0], g_mix[0], g_ffn[0])):
                row(0, (9 + v) * KT, src, KT)
            act.dma_start(rows[0:CK * RT, 1, :],
                          conv_w[0].rearrange("t (r p) -> (t r) p", p=P)).then_inc(rows_loaded, 16)
            for v, src in enumerate((conv_b[0], conv_ln_g[0], conv_ln_b[0], w0[0], a0[0], k_k[0], k_a[0],
                                     r_k[0].rearrange("h n -> (h n)"), gn_g[0], gn_b[0])):
                row(2, v * RT, src, RT)
            row(2, 10 * RT, mu_shift[0], ZT)

            def norm(j, split_at=None):
                c = norm_cols(j)
                for kt in range(KT):
                    act.wait_ge(x_ready, KT * j + kt + 1)
                    a.activation(sq[:, kt, c], xT[:, kt, c], ACT.Square).then_inc(sq_ready, 1)
                    if split_at is not None:
                        act.wait_ge(xg_ready, split_at + kt + 1)
                        a.activation(x_hl[0][:, kt, :], hT[:, kt, real], ACT.Copy).then_inc(x_high, 1)
                act.wait_ge(mean_ready, j + 1)
                n = c.stop - c.start
                a.activation(rs[:, 0:n], rtmp[:, 0:n], ACT.Sqrt).then_inc(rs_ready, 1)

            def split_high(layer, i, j):
                s = SLOTS[f"up{layer}"] + j // 2
                if j % 2 == 0:
                    act.wait_ge(w_loaded[s % RING], i * 16 + 16 * (s // RING + 1))
                if j >= UNITS:
                    act.wait_ge(group_done, i * 8 + (plan.at[f"up{layer}"][0] + j - UNITS + 1))
                a.activation(w_hl[0][:, j % UNITS], raw_unit(j), ACT.Copy).then_inc(w_high, 1)

            def split_weights(layer):
                with act.Fori(0, MLP_UNITS // 8 - 1, 1) as i:
                    for j in range(UNITS, UNITS + 8):
                        split_high(layer, i, j)
                for j in range(UNITS):
                    split_high(layer, 0, MLP_UNITS - UNITS + j)

            norm(0)
            for m in range(KT):
                pb = wait_group(act, f"q{m}")
                a.activation(qT[:, m, :], pb[:, 0:SEQ], ACT.Copy, scale=HD ** -0.5).then_inc(free(f"q{m}"), 1)
            a.preload_act_table_set("natural_log_exp_and_others")
            for i in range(HEADS + 1):
                if i < HEADS:
                    pb = wait_group(act, f"z{i}")
                    if i >= 2:
                        act.wait_ge(sp_ready, i - 1)
                    t = lnz[:, i % 2, :]
                    link(a.activation(t, pb[:, 0:384], ACT.Abs))
                    link(a.activation(t, t, ACT.Exp, scale=-1.0))
                    a.activation(t, t, ACT.Ln, bias=1.0).then_inc(lnz_ready, 1)
                if i >= 1:
                    h = i - 1
                    act.wait_ge(cum_done, h + 1)
                    if h >= 2:
                        if h % 2:
                            wait_group(act, f"o{(h - 2) // 2}")
                        else:
                            act.wait_ge(o_done, h // 2)
                    a.activation(wexp[:, h % 2, :], bank[plan.at[f"z{h}"][1]][:, 0:384],
                                 ACT.Exp).then_inc(free(f"z{h}"), 1)
            for j in range(UNITS):
                split_high(0, 0, j)
            norm(1, split_at=0)
            split_weights(0)
            wait_out(act, "par")
            lam = par[:, 12 * KT:13 * KT]
            link(a.activation(lamc[:, 0, :], lam, ACT.Abs))
            link(a.activation(lamc[:, 1, :], lamc[:, 0, :], ACT.Exp, scale=-1.0))
            a.activation(lamc[:, 2, :], lamc[:, 1, :], ACT.Ln, bias=1.0).then_inc(lam_ready, 1)
            norm(2)
            act.wait_ge(xc_ready, 1)
            for m in range(KT):
                pb = wait_group(act, f"rg{m}")
                a.activation(xraw[:, m, CONV - 1:], pb[:, 0:SEQ], ACT.Copy).then_inc(free(f"rg{m}"), 1)
            for m in range(KT):
                pb = wait_group(act, f"rg{KT + m}")
                a.activation(gate[:, m, :], pb[:, 0:SEQ], ACT.Gelu_apprx_tanh).then_inc(free(f"rg{KT + m}"), 1)
            for m in range(KT):
                pb = wait_group(act, f"ri{m}")
                a.activation(rS[:, m, :], pb[:, 0:SEQ], ACT.Sigmoid,
                             bias=par[:, 10 * KT + m:10 * KT + m + 1]).then_inc(ri_ready, 1)
                a.activation(iS[:, m, :], pb[:, SEQ:2 * SEQ], ACT.Sigmoid,
                             bias=par[:, 11 * KT + m:11 * KT + m + 1]).then_inc(free(f"ri{m}"), 1)
            act.wait_ge(ri_ready, KT)
            act.wait_ge(lam_ready, 2)
            for m in range(KT):
                a.activation(aS[:, m, :], rS[:, m, :], ACT.Exp, scale=lamc[:, 4, m:m + 1]).then_inc(at_ready, 1)
                a.activation(tS[:, m, :], rS[:, m, :], ACT.Tanh, scale=lamc[:, 3, m:m + 1]).then_inc(at_ready, 1)
            act.wait_ge(m_ready, 1)
            a.activation(mS, mS, ACT.Sqrt).then_inc(mroot_ready, 1)
            act.wait_ge(y_ready, 1)
            for j in range(UNITS):
                split_high(1, 0, j)
            norm(3, split_at=KT)
            split_weights(1)
            norm(4)
            norm(5)
            act.wait_ge(zf_ready, 1)
            for m in range(ZT):
                pb = wait_group(act, f"zr{m}")
                a.activation(zr[:, m, 1:], pb[:, 0:TOK], ACT.Copy).then_inc(free(f"zr{m}"), 1)
            for m in range(RT):
                pb = wait_group(act, f"val{m}")
                a.activation(val[:, m, :], pb[:, 0:TOK], ACT.Copy).then_inc(free(f"val{m}"), 1)
            for m in range(RT):
                pb = wait_group(act, f"cg{m}")
                a.activation(cg[:, m, :], pb[:, 0:TOK], ACT.Sigmoid).then_inc(free(f"cg{m}"), 1)
            act.wait_ge(zf_ready, 2)
            a.activation(tlw[0:64], zf[0:64, 12, :], ACT.Tanh).then_inc(lw_ready, 1)
            a.activation(slg, zf[:, 13, CH:WT], ACT.Sigmoid).then_inc(lw_ready, 1)
            for m in range(RT):
                pb = wait_group(act, f"wp{m}")
                a.activation(ld[:, m, :], pb[:, 0:WT], ACT.Sigmoid,
                             bias=par[:, 268 + m:269 + m]).then_inc(free(f"wp{m}"), 1)
            for m in range(RT):
                pb = wait_group(act, f"ap{m}")
                a.activation(aa[:, m, :], pb[:, 0:WT], ACT.Sigmoid,
                             bias=par[:, 272 + m:273 + m]).then_inc(free(f"ap{m}"), 1)
            act.wait_ge(kkn_ready, 1)
            a.activation(Kh, Bh, ACT.Sqrt).then_inc(ksq_ready, 1)
            act.wait_ge(lp_ready, 1)
            link(a.activation(Pd, LP, ACT.Exp))
            link(a.activation(Pi, LP, ACT.Exp, scale=-1.0))
            act.wait_ge(lp_ready, 2)
            a.activation(ld, ld, ACT.Exp).then_inc(p_ready, 1)
            for tt in range(3):
                n = CH if tt == 0 else P
                for s_ in range(3):
                    pb = wait_group(act, f"nat{s_}_{tt}")
                    a.activation(nat[s_][0:n, tt, :], pb[0:n, :], ACT.Copy,
                                 scale=-1.0 if s_ == 2 else 1.0).then_inc(free(f"nat{s_}_{tt}"), 1)
            for lv in range(1, LEVELS):
                for tt in range(3):
                    n = CH if tt == 0 else P
                    pb = wait_group(act, f"Y{lv}_{tt}")
                    a.activation(Y[0:n, tt].rearrange("p h s -> p (h s)"), pb[0:n, :],
                                 ACT.Copy).then_inc(free(f"Y{lv}_{tt}"), 1)
            for tt in range(3):
                n = CH if tt == 0 else P
                pb = wait_group(act, f"GV_{tt}")
                a.activation(G1[0:n, tt].rearrange("p h s -> p (h s)"), pb[0:n, :], ACT.Copy).then_inc(free(f"GV_{tt}"), 1)
            for c in range(NCH):
                p0 = CH * ((c - 1) % 2) if c else 0
                pb = wait_group(act, f"U_{c}")
                a.activation(Uc[p0:p0 + CH].rearrange("p h v -> p (h v)"), pb[p0:p0 + CH, :], ACT.Copy).then_inc(free(f"U_{c}"), 1)
                if c:
                    pb = wait_group(act, f"OA_{c}")
                    a.activation(owk[:, :, (c - 1) * CH:c * CH],
                                      pb[:, 0:RT * CH].rearrange("p (q t) -> p q t", t=CH), ACT.Copy).then_inc(free(f"OA_{c}"), 1)
            act.wait_ge(osq_ready, 2)
            a.activation(orr, orr, ACT.Sqrt).then_inc(rs_ready, 1)
            for m in range(2 * KT):
                pb = wait_group(act, f"gl{m}")
                a.activation(GAB[:, m, :], pb[:, 0:SEQ], ACT.Sigmoid).then_inc(free(f"gl{m}"), 1)
            act.wait_ge(csq_ready, 2)
            a.activation(rs[:, 0:SEQ], rtmp[:, 0:SEQ], ACT.Sqrt).then_inc(rs_ready, 1)
            act.wait_ge(cin_ready, 1)
            a.activation(ct, cy, ACT.Sigmoid).then_inc(cin_sig, 1)
            norm(6)
            for m in range(2 * PH):
                pb = wait_group(act, f"pq{m}")
                a.activation(pq[:, m, :], pb[:, 0:SEQ], ACT.Copy).then_inc(free(f"pq{m}"), 1)
            for tt in range(2):
                for dst, nm in ((fnat, "xn"), (hnat, "hn")):
                    for m in range(2):
                        pb = wait_group(act, f"{nm}{tt}_{m}")
                        a.activation(dst[:, tt, 512 * m:512 * (m + 1)], pb[:, :], ACT.Copy).then_inc(free(f"{nm}{tt}_{m}"), 1)
            for tt in range(2):
                for m in range(4):
                    act.wait_ge(gsel_ready, 4 * tt + m + 1)
                    g3 = gsel[:, tt, 2 * TOPK * m:2 * TOPK * (m + 1)]
                    a.activation(g3, g3, ACT.Exp).then_inc(gsel_exp, 1)
            act.wait_ge(eidx_ready, 2)
            act.dma_start(gfin, g_final.partition_broadcast(P)).then_inc(gfin_loaded, 16)
            for tt in range(2):
                act.wait_ge(dots_ready, tt + 1)
                a.activation(coef[:, tt, :], dots[:, tt, :], ACT.Gelu).then_inc(gelu_ready, 1)
                act.wait_ge(y_ready2, 2 * tt + 1)
                a.activation(junk, yacc, ACT.Square, accum_out=fsq[:, 0:1]).then_inc(fsum_ready, 1)
                act.wait_ge(y_ready2, 2 * tt + 2)
                a.activation(fsq[:, 2:3], fsq[:, 1:2], ACT.Sqrt).then_inc(fsum_ready, 1)

        @block.vector
        def _(dve):
            chain = [0]
            v = nc.vector

            def link(ins):
                chain[0] += 1
                ins.then_inc(dve_chain, 1)
                dve.wait_ge(dve_chain, chain[0])

            def mark(ins):
                chain[0] += 1
                ins.then_inc(dve_chain, 1)

            def settle():
                dve.wait_ge(dve_chain, chain[0])

            def pc(i, m):
                return par[:, i * KT + m:i * KT + m + 1]

            def pr(i, m):
                return par[:, 256 + RT * i + m:257 + RT * i + m]

            def norm(j, gain, dst=hT):
                c = norm_cols(j)
                n = c.stop - c.start
                pb = wait_group(dve, f"ms{j}")
                link(v.tensor_scalar(rtmp[:, 0:n], pb[:, 0:n], EPS, None, ALU.add))
                link(v.reciprocal(rtmp[:, 0:n], rtmp[:, 0:n]))
                dve.sem_inc(free(f"ms{j}"), 1)
                dve.sem_inc(mean_ready, 1)
                dve.wait_ge(rs_ready, RS_AT[j])
                if gain is None:
                    return
                for kt in range(KT):
                    ins = v.scalar_tensor_tensor(dst[:, kt, c], xT[:, kt, c], pc(gain, kt), rs[:, 0:n],
                                                 ALU.mult, ALU.mult)
                    ins.then_inc(h_ready if dst is hT else x_ready, 1)

            def residual(names, gain=None):
                for kt, name in enumerate(names):
                    pb = wait_group(dve, name)
                    link(v.tensor_tensor(xT[:, kt, real], xT[:, kt, real], pb[:, 0:SEQ], ALU.add))
                    dve.sem_inc(free(name), 1)
                    dve.sem_inc(x_ready, 1)
                    if gain is not None:
                        v.tensor_scalar(hT[:, kt, real], xT[:, kt, real], pc(gain, kt), None,
                                        ALU.mult).then_inc(xg_ready, 1)
                for kt in range(KT if gain is not None else 0):
                    dve.wait_ge(x_high, KT * (gain - 2) + kt + 1)
                    v.tensor_tensor(x_hl[1][:, kt, :], hT[:, kt, real], x_hl[0][:, kt, :].bitcast(F32),
                                    ALU.subtract).then_inc(h_ready, 1)

            for kt in range(KT):
                pb = wait_group(dve, f"xT{kt}")
                link(v.tensor_copy(xT[:, kt, :], pb[:, 0:TOK]))
                dve.sem_inc(free(f"xT{kt}"), 1)
                dve.sem_inc(x_ready, 1)
            pb = wait_group(dve, "par")
            mark(v.tensor_copy(par[:, 0:15 * KT], pb[:, 0:15 * KT]))
            mark(v.tensor_copy(par[:, 128:128 + CK * RT], pb[:, 128:128 + CK * RT]))
            mark(v.tensor_copy(par[:, 256:256 + 10 * RT + ZT], pb[:, 256:256 + 10 * RT + ZT]))
            settle()
            dve.sem_inc(free("par"), 1)
            norm(0, 0)
            for m in range(KT):
                pb = wait_group(dve, f"k{m}")
                v.tensor_copy(kT[:, m, :], pb[:, 0:SEQ]).then_inc(free(f"k{m}"), 1)
            for j in range(4):
                for tt in range(2):
                    pb = wait_group(dve, f"v{j}_{tt}")
                    v.tensor_copy(V[:, tt, 256 * j:256 * (j + 1)], pb[:, 0:256]).then_inc(free(f"v{j}_{tt}"), 1)
            dve.wait_ge(consts_built, 2)
            for i in range(HEADS + 3):
                if i < HEADS:
                    dve.wait_ge(lnz_ready, i + 1)
                    if i >= 2:
                        dve.wait_ge(cum_done, i - 1)
                    link(v.scalar_tensor_tensor(sp[:, i % 2, :], bank[plan.at[f"z{i}"][1]][:, 0:384], 0.0,
                                                lnz[:, i % 2, :], ALU.max, ALU.add))
                    v.tensor_tensor(sp[:, i % 2, :], sp[:, i % 2, :], attn_mask[:], ALU.mult).then_inc(sp_ready, 1)
                if 1 <= i <= HEADS:
                    h = i - 1
                    wait_out(dve, f"z{h}")
                    v.scalar_tensor_tensor(wexp[:, h % 2, :], wexp[:, h % 2, :], 2.0, attn_mask[:],
                                           ALU.min, ALU.mult).then_inc(w_ready, 1)
                if i >= 3 and i % 2 == 1:
                    q = (i - 3) // 2
                    pb = wait_group(dve, f"o{q}")
                    v.tensor_copy(oT[:, q, :], pb[:, 0:SEQ]).then_inc(free(f"o{q}"), 1)
            residual([f"wo{m}" for m in range(KT)], gain=2)

            def mlp(layer):
                n0, banks, used = plan.at[f"up{layer}"]
                with dve.Fori(0, 4, 1) as i:
                    for j in range(BANKS):
                        dve.wait_ge(group_done, i * BANKS + (n0 + j + 1))
                        def step(k):
                            dve.wait_ge(u_step, i * (3 * BANKS) + (3 * (FF // P * layer + j) + k))

                        t, u_ = utmp[:, j % 2, :], utmp[:, 2 + j % 2, :]
                        high, low = (u_hl[part][:, bass.ds(i * BANKS + j, 1), :].rearrange("p a b -> p (a b)")
                                     for part in range(2))
                        v.scalar_tensor_tensor(t, bank[banks[j]][:, 0:SEQ], 0.0, rs[:, 0:SEQ], ALU.max,
                                               ALU.mult).then_inc(bank_free[banks[j]], 1)
                        dve.wait_ge(bank_free[banks[j]], i + (used[j] + 1))
                        v.tensor_tensor(u_, t, t, ALU.mult).then_inc(u_step, 1)
                        step(1)
                        v.tensor_copy(high, u_).then_inc(u_step, 1)
                        step(2)
                        v.tensor_tensor(low, u_, high.bitcast(F32), ALU.subtract).then_inc(u_step, 1)
                n0, banks, used = plan.at[f"down{layer}"]
                with dve.Fori(0, 4, 1) as i:
                    for j in range(2):
                        dve.wait_ge(group_done, i * 8 + (n0 + 6 + j + 1))
                        xs = xT[:, i * 2 + j, real]
                        v.tensor_tensor(xs, xs, bank[banks[j]][:, 0:SEQ], ALU.add).then_inc(x_ready, 1)
                        dve.wait_ge(x_ready, i * 2 + (KT * (2 + 2 * layer) + j + 1))
                        dve.sem_inc(bank_free[banks[j]], 1)

            norm(1, None)
            mlp(0)
            dve.wait_ge(lam_ready, 1)
            link(v.tensor_scalar(lamc[:, 3, :], par[:, 12 * KT:13 * KT], -1.0, 0.0, ALU.mult, ALU.max))
            link(v.tensor_tensor(lamc[:, 3, :], lamc[:, 3, :], lamc[:, 2, :], ALU.add))
            link(v.tensor_scalar(lamc[:, 3, :], lamc[:, 3, :], 8.0, None, ALU.mult))
            link(v.tensor_scalar(lamc[:, 4, :], lamc[:, 3, :], -1.0, None, ALU.mult))
            dve.sem_inc(lam_ready, 1)
            v.memset(xraw[:, :, 0:CONV - 1], 0.0).then_inc(xc_ready, 1)
            norm(2, 1)
            for m in range(KT):
                wait_out(dve, f"rg{m}")
                link(v.tensor_scalar(xc[:, m, :], xraw[:, m, 0:SEQ], pc(5, m), pc(9, m), ALU.mult, ALU.add))
                for t in range(1, CONV):
                    link(v.scalar_tensor_tensor(xc[:, m, :], xraw[:, m, t:t + SEQ], pc(5 + t, m),
                                                xc[:, m, :], ALU.mult, ALU.add))
                dve.sem_inc(xc_ready, 1)
            dve.wait_ge(at_ready, 2 * KT)
            link(v.tensor_scalar(mS, tS, 1.0, None, ALU.add))
            link(v.reciprocal(mS, mS))
            link(v.scalar_tensor_tensor(mS.rearrange("p a b -> p (a b)"), tS.rearrange("p a b -> p (a b)"), 2.0,
                                        mS.rearrange("p a b -> p (a b)"), ALU.mult, ALU.mult))
            dve.sem_inc(m_ready, 1)
            wait_out(dve, *[f"ri{m}" for m in range(KT)])
            link(v.tensor_tensor(iS, iS, xc, ALU.mult))
            dve.wait_ge(mroot_ready, 1)
            link(v.tensor_tensor(iS, iS, mS, ALU.mult))
            for m in range(KT):
                mark(v.tensor_tensor_scan(rS[:, m, :], aS[:, m, :], iS[:, m, :], 0.0, ALU.mult, ALU.add))
            settle()
            wait_out(dve, *[f"rg{KT + m}" for m in range(KT)])
            v.tensor_tensor(gate, gate, rS, ALU.mult).then_inc(y_ready, 1)
            residual([f"rgo{m}" for m in range(KT)], gain=3)
            norm(3, None)
            mlp(1)
            norm(4, 4, xT)
            v.memset(zf[:, :, 0:PADC], 0.0).then_inc(dve_chain, 1)
            chain[0] += 1
            mark(v.memset(U[:, :, 0:CK - 1], 0.0))
            mark(v.memset(zr[:, :, 0:1], 0.0))
            settle()
            dve.sem_inc(zf_ready, 1)
            norm(5, 13)
            for m in range(ZT):
                wait_out(dve, f"zr{m}")
                z = zf[:, m, PADC:]
                link(v.tensor_tensor(z, zr[:, m, 0:TOK], zr[:, m, 1:], ALU.subtract))
                mark(v.scalar_tensor_tensor(z, z, par[:, 296 + m:297 + m], zr[:, m, 1:], ALU.mult, ALU.add))
            settle()
            dve.sem_inc(zf_ready, 1)
            for m in range(RT):
                mark(v.tensor_scalar(kk[:, m, :], kZ[:, m, :], pr(5, m), None, ALU.mult))
            settle()
            v.tensor_tensor(Kh, kk, kk, ALU.mult).then_inc(kks_ready, 1)
            link(v.tensor_scalar(omka[:], par[:, 280:284], -1.0, 1.0, ALU.mult, ALU.add))
            wait_out(dve, *[f"val{m}" for m in range(RT)], *[f"cg{m}" for m in range(RT)])
            link(v.tensor_tensor(U[:, :, CK - 1:], val, cg, ALU.mult))
            for m in range(RT):
                pb = wait_group(dve, f"kks{m}")
                v.tensor_scalar(Bh[:, m, :], pb[:, 0:WT], 1e-24, None, ALU.max).then_inc(free(f"kks{m}"), 1)
            wait_out(dve, *[f"kks{m}" for m in range(RT)])
            link(v.reciprocal(Bh, Bh))
            dve.sem_inc(kkn_ready, 1)
            wait_out(dve, *[f"wp{m}" for m in range(RT)])
            link(v.tensor_scalar(ld, ld, DECAY, None, ALU.mult))
            for m in range(RT):
                mark(v.tensor_tensor_scan(LP[:, m, :], reset[:], ld[:, m, :], 0.0, ALU.mult, ALU.add))
            settle()
            dve.sem_inc(lp_ready, 1)
            link(v.tensor_tensor(ld, LP, ld, ALU.subtract))
            dve.sem_inc(lp_ready, 1)
            dve.wait_ge(ksq_ready, 1)
            link(v.tensor_tensor(kk, kk, Kh, ALU.mult))
            wait_out(dve, *[f"ap{m}" for m in range(RT)])
            for m in range(RT):
                mark(v.tensor_scalar(Bh[:, m, :], aa[:, m, :], pr(6, m), omka[:, m:m + 1], ALU.mult, ALU.add))
            settle()
            link(v.tensor_tensor(kZ, kZ, Bh, ALU.mult))
            link(v.tensor_tensor(Kh, rZ, kZ, ALU.mult))
            for m in range(RT):
                mark(v.tensor_scalar(Kh[:, m, :], Kh[:, m, :], pr(7, m), None, ALU.mult))
            settle()
            dve.sem_inc(rk_ready, 1)
            for m in range(RT):
                pb = wait_group(dve, f"gp{m}")
                v.tensor_copy(gg[:, m, :], pb[:, 0:SEQ]).then_inc(free(f"gp{m}"), 1)
            for m in range(RT):
                pb = wait_group(dve, f"bon{m}")
                v.tensor_tensor(bonus[:, m, :], vZ[:, m, CH:WT], pb[:, 0:SEQ], ALU.mult).then_inc(free(f"bon{m}"), 1)
            wait_out(dve, *[f"bon{m}" for m in range(RT)])
            dve.wait_ge(p_ready, 1)
            mark(v.tensor_tensor(aa, aa, kk, ALU.mult))
            mark(v.tensor_tensor(rZ, rZ, Pd, ALU.mult))
            mark(v.tensor_tensor(kZ, kZ, Pi, ALU.mult))
            settle()
            mark(v.tensor_tensor(aa, aa, Pi, ALU.mult))
            mark(v.tensor_tensor(kk, kk, ld, ALU.mult))
            ends = Pd.rearrange("p m (c j) -> p (m c) j", j=CH)[:, :, CH - 1:CH]
            mark(v.tensor_copy(pend[:].rearrange("p m c -> p (m c)").unsqueeze(2), ends))
            settle()

            def chunks(t):
                return t.rearrange("p m (c j) -> p (m c) j", j=CH)

            pend_b = pend[:].rearrange("p m c -> p (m c)").unsqueeze(2).broadcast_to([P, RT * NCH, CH])
            mark(v.tensor_tensor(chunks(Kh), chunks(kZ), pend_b, ALU.mult))
            mark(v.tensor_tensor(chunks(Bh), chunks(aa), pend_b, ALU.mult))
            settle()
            dve.sem_inc(kb_ready, 1)
            wait_out(dve, *[f"nat{s_}_{tt}" for tt in range(3) for s_ in range(3)])
            for tt in range(3):
                n = CH if tt == 0 else P
                for s_ in range(5 if tt else 3):
                    dst, mask = ((NT[0:n, tt], strict), (Nm[0:n, tt], lower), (G1[0:n, tt], strict),
                                 (G2[0:n, max(tt - 1, 0)], incl), (G3[0:n, max(tt - 1, 0)], nincl))[s_]
                    dst = dst.rearrange("p (q two) t -> p two q t", two=2)
                    for par_ in range(2):
                        pb = wait_group(dve, f"mat{s_}_{par_}_{tt}")
                        v.tensor_tensor(dst[:, par_], pb[0:n, 0:256].rearrange("p (q t) -> p q t", t=CH),
                                        mask[0:n].unsqueeze(1).broadcast_to([n, 4, CH]),
                                        ALU.mult).then_inc(free(f"mat{s_}_{par_}_{tt}"), 1)
                wait_out(dve, *[f"mat{s_}_{par_}_{tt}" for s_ in range(2) for par_ in range(2)])

            def block_of(dst, src, which, tt):
                n = CH if tt == 0 else P
                return v.tensor_tensor(dst[0:n, tt], src[0:n, tt],
                                       lvl[0:n, which, :].unsqueeze(1).broadcast_to([n, RH, CH]), ALU.mult)

            for tt in range(3):
                n = CH if tt == 0 else P
                eye_b = eye[0:n].unsqueeze(1).broadcast_to([n, RH, CH])
                for dst, src, which in ((X, Nm, 0), (XT, NT, LEVELS)):
                    link(block_of(dst, src, which, tt))
                    link(v.tensor_tensor(dst[0:n, tt], eye_b, dst[0:n, tt], ALU.subtract))
                link(block_of(MT, NT, LEVELS + 1, tt))
                dve.sem_inc(mt_ready, 1)
            for lv in range(1, LEVELS):
                for tt in range(3):
                    n = CH if tt == 0 else P
                    if lv < LEVELS - 1:
                        pb = wait_group(dve, f"XY{lv}_{tt}")
                        xx = X[0:n, tt].rearrange("p h s -> p (h s)")
                        v.tensor_tensor(xx, xx, pb[0:n, :], ALU.subtract).then_inc(free(f"XY{lv}_{tt}"), 1)
                    pb = wait_group(dve, f"YX{lv}_{tt}")
                    xx = XT[0:n, tt].rearrange("p h s -> p (h s)")
                    v.tensor_tensor(xx, xx, pb[0:n, :], ALU.subtract).then_inc(free(f"YX{lv}_{tt}"), 1)
                    if lv < LEVELS - 1:
                        link(block_of(MT, NT, LEVELS + lv + 1, tt))
                        dve.sem_inc(mt_ready, 1)
            dve.wait_ge(group_done, plan.at["GV_2"][0])
            wait_out(dve, *[f"GV_{tt}" for tt in range(3)])
            for c in range(NCH):
                tt = (c + 1) // 2
                p0 = CH * ((c - 1) % 2) if c else 0
                rows_ = slice(p0, p0 + CH)
                if c == 0:
                    link(v.tensor_copy(Yc[rows_], G1[rows_, 0]))
                else:
                    for par_ in range(2):
                        pb = wait_group(dve, f"SA{par_}_{c}")
                        yv = Yc[rows_].rearrange("p (q two) t -> p two q t", two=2)[:, par_]
                        gv = G1[rows_, tt].rearrange("p (q two) t -> p two q t", two=2)[:, par_]
                        link(v.tensor_tensor(yv, gv, pb[rows_, 0:256].rearrange("p (q t) -> p q t", t=CH), ALU.add))
                        dve.sem_inc(free(f"SA{par_}_{c}"), 1)
                dve.sem_inc(yc_ready, 1)
                new, old = ST[:, (c + 1) % 2], ST[:, c % 2]
                if c:
                    link(v.tensor_tensor(new, old, pend[:, :, c:c + 1].broadcast_to([P, RT, CH]), ALU.mult))
                pb = wait_group(dve, f"S_{c}")
                pv = pb[:, 0:RT * CH].rearrange("p (q t) -> p q t", t=CH)
                if c:
                    link(v.tensor_tensor(new, new, pv, ALU.add))
                else:
                    link(v.tensor_copy(new, pv))
                dve.sem_inc(free(f"S_{c}"), 1)
                dve.sem_inc(st_ready, 1)
                if c:
                    pb = wait_group(dve, f"OB_{c}")
                    wait_out(dve, f"OA_{c}")
                    ov = owk[:, :, (c - 1) * CH:c * CH]
                    link(v.tensor_tensor(ov, ov, pb[:, 0:RT * CH].rearrange("p (q t) -> p q t", t=CH), ALU.add))
                    dve.sem_inc(free(f"OB_{c}"), 1)
            dve.sem_inc(owk_ready, 1)
            for m in range(RT):
                pb = wait_group(dve, f"gm{m}")
                link(v.tensor_tensor(owk[:, m, :], owk[:, m, :], pb[:, 0:SEQ], ALU.subtract))
                dve.sem_inc(free(f"gm{m}"), 1)
            link(v.tensor_tensor(osq, owk, owk, ALU.mult))
            dve.sem_inc(osq_ready, 1)
            for m in range(RT):
                pb = wait_group(dve, f"gv{m}")
                link(v.tensor_scalar(orr[:, m, :], pb[:, 0:SEQ], GN_EPS, None, ALU.add))
                dve.sem_inc(free(f"gv{m}"), 1)
            link(v.reciprocal(orr, orr))
            dve.sem_inc(osq_ready, 1)
            for t in range(CK):
                settle()
                for m in range(RT):
                    u_ = U[:, m, META + t:META + t + SEQ]
                    w_ = par[:, 128 + RT * t + m:129 + RT * t + m]
                    if t == 0:
                        mark(v.tensor_scalar(cy[:, m, :], u_, w_, pr(0, m), ALU.mult, ALU.add))
                    else:
                        mark(v.scalar_tensor_tensor(cy[:, m, :], u_, w_, cy[:, m, :], ALU.mult, ALU.add))
            settle()
            dve.sem_inc(cy_ready, 1)
            dve.wait_ge(rs_ready, RS_AT["gn"])
            link(v.tensor_tensor(owk, owk, orr, ALU.mult))
            for m in range(RT):
                mark(v.tensor_scalar(owk[:, m, :], owk[:, m, :], pr(8, m), pr(9, m), ALU.mult, ALU.add))
            settle()
            link(v.tensor_tensor(owk, owk, bonus, ALU.add))
            link(v.tensor_tensor(owk, owk, gg, ALU.mult))
            dve.sem_inc(yb_in, 1)
            pb = wait_group(dve, "lm")
            link(v.tensor_tensor(cy, cy, pb[:, 0:SEQ].unsqueeze(1).broadcast_to([P, RT, SEQ]), ALU.subtract))
            dve.sem_inc(free("lm"), 1)
            link(v.tensor_tensor(ct, cy, cy, ALU.mult))
            dve.sem_inc(csq_ready, 1)
            pb = wait_group(dve, "lv")
            link(v.tensor_scalar(rtmp[:, 0:SEQ], pb[:, 0:SEQ], LN_EPS, None, ALU.add))
            link(v.reciprocal(rtmp[:, 0:SEQ], rtmp[:, 0:SEQ]))
            dve.sem_inc(free("lv"), 1)
            dve.sem_inc(csq_ready, 1)
            dve.wait_ge(rs_ready, RS_AT["ln"])
            link(v.tensor_tensor(cy, cy, rs[:, 0:SEQ].unsqueeze(1).broadcast_to([P, RT, SEQ]), ALU.mult))
            for m in range(RT):
                mark(v.tensor_scalar(cy[:, m, :], cy[:, m, :], pr(1, m), pr(2, m), ALU.mult, ALU.add))
            settle()
            dve.sem_inc(cin_ready, 1)
            dve.wait_ge(cin_sig, 1)
            link(v.tensor_tensor(cy, cy, ct, ALU.mult))
            dve.sem_inc(cin_sig, 1)
            wait_out(dve, *[f"gl{m}" for m in range(2 * KT)][KT:])
            for m in range(KT):
                pb = wait_group(dve, f"yb{m}")
                v.tensor_tensor(mix[:, m, :], pb[:, 0:SEQ], GAB[:, KT + m, :], ALU.mult).then_inc(free(f"yb{m}"), 1)
            for m in range(KT):
                pb = wait_group(dve, f"ya{m}")
                link(v.tensor_tensor(mt2, pb[:, 0:SEQ], GAB[:, m, :], ALU.mult))
                dve.sem_inc(free(f"ya{m}"), 1)
                v.tensor_tensor(mix[:, m, :], mix[:, m, :], mt2, ALU.add).then_inc(mix_ready, 1)
                dve.wait_ge(mix_ready, m + 1)
            residual([f"wo2{m}" for m in range(KT)])
            norm(6, 14)
            for m in range(4):
                pb = wait_group(dve, f"key{m}")
                v.tensor_copy(keyT[:, 4 * m:4 * m + 4, :].rearrange("p a n -> p (a n)"),
                              pb[:, :]).then_inc(free(f"key{m}"), 1)

            def top16(vals, idx, src, rest):
                for r_ in range(src.shape[1]):
                    mark(v.max(vals[:, r_, 0:8], src[:, r_, :]))
                settle()
                for r_ in range(src.shape[1]):
                    mark(v.max_index(idx[:, r_, 0:8], vals[:, r_, 0:8], src[:, r_, :]))
                    mark(v.match_replace(rest[:, r_, :], vals[:, r_, 0:8], src[:, r_, :], NEG))
                settle()
                for r_ in range(src.shape[1]):
                    mark(v.max(vals[:, r_, 8:16], rest[:, r_, :]))
                settle()
                for r_ in range(src.shape[1]):
                    mark(v.max_index(idx[:, r_, 8:16], vals[:, r_, 8:16], rest[:, r_, :]))
                settle()

            def choose(tt, m):
                hs, hc = slice(2 * m, 2 * m + 2), slice(4 * m, 4 * m + 4)
                pb = wait_group(dve, f"sc{tt}_{m}")
                link(v.tensor_copy(sc[:, hc, :].rearrange("p a n -> p (a n)"), pb[:, :]))
                dve.sem_inc(free(f"sc{tt}_{m}"), 1)
                top16(topv[:, hc], topi[:, hc], sc[:, hc], sc2[:, hc])
                mark(v.tensor_copy(topf[:, hc], topi[:, hc]))
                for h in (2 * m, 2 * m + 1):
                    mark(v.tensor_tensor(cand[:, h, :].rearrange("p (i j) -> p i j", j=TOPK),
                                         topv[:, 2 * h, :].unsqueeze(2).broadcast_to([P, TOPK, TOPK]),
                                         topv[:, 2 * h + 1, :].unsqueeze(1).broadcast_to([P, TOPK, TOPK]), ALU.add))
                settle()
                top16(bv[:, hs], bi[:, hs], cand[:, hs], cand2[:, hs])
                g3 = gsel[:, tt, :].rearrange("p (h s) -> p h s", s=TOPK)[:, hs]
                link(v.tensor_tensor(g3, bv[:, hs], bv[:, hs, 0:1].broadcast_to([P, 2, TOPK]), ALU.subtract))
                dve.sem_inc(gsel_ready, 1)
                mark(v.tensor_scalar(bt[:, hs], bi[:, hs], 4, None, ALU.logical_shift_right))
                mark(v.tensor_scalar(bt2[:, hs], bi[:, hs], TOPK - 1, None, ALU.bitwise_and))
                settle()
                mark(v.tensor_copy(rowf[:, hs], bt[:, hs]))
                mark(v.tensor_copy(colf[:, hs], bt2[:, hs]))
                settle()
                n = 2 * TOPK
                for src, half, dst in ((rowf, 0, i1f), (colf, 1, i2f)):
                    o_ = oh[:, n * m:n * (m + 1), :]
                    link(v.tensor_tensor(o_, src[:, hs].rearrange("p h s -> p (h s)").unsqueeze(2).broadcast_to([P, n, TOPK]),
                                         io16[:].unsqueeze(1).broadcast_to([P, n, TOPK]), ALU.is_equal))
                    for h in range(2):
                        oo = o_[:, TOPK * h:TOPK * (h + 1), :]
                        mark(v.tensor_tensor(oo, oo, topf[:, 4 * m + 2 * h + half, :].unsqueeze(1).broadcast_to(
                            [P, TOPK, TOPK]), ALU.mult))
                    settle()
                    link(v.tensor_reduce(dst[:, hs].rearrange("p h s -> p (h s)"), o_, AX.X, ALU.add))
                i1, i2 = (t[:, hs].rearrange("p h s -> p (h s)") for t in (i1f, i2f))
                link(v.scalar_tensor_tensor(i1, i1, float(NK), i2, ALU.mult, ALU.add))
                link(v.tensor_copy(eidx[:, tt, n * m:n * (m + 1)], i1))

            def share(tt):
                g3 = gsel[:, tt, :].rearrange("p (h s) -> p h s", s=TOPK)
                dve.wait_ge(gsel_exp, 4 * (tt + 1))
                link(v.tensor_reduce(psm, g3, AX.X, ALU.add))
                link(v.reciprocal(psm, psm))
                link(v.tensor_tensor(g3, g3, psm.unsqueeze(2).broadcast_to([P, PH, TOPK]), ALU.mult))

            dve.wait_ge(io_ready, 1)
            for m in range(4):
                choose(0, m)
            dve.sem_inc(rows_free, GR)
            dve.sem_inc(eidx_ready, 1)

            def dot_rounds(tt, r0, count):
                first = 2 * tt * (SEL // GR) + r0
                with dve.Fori(0, count, 1) as i:
                    for j in range(GR):
                        dve.wait_ge(row_loaded[j], i * 16 + 16 * (first + 1))
                        v.tensor_tensor_reduce(out=junk, in0=grow(j), in1=fnat[:, tt, :], scale=1.0, scalar=0.0,
                                               op0=ALU.mult, op1=ALU.add,
                                               accum_out=dot16[:, j:j + 1]).then_inc(rows_free, 1)
                        dve.wait_ge(rows_free, i * GR + (GR * (first + 1) + j + 1))
                    v.tensor_copy(dots[:, tt, bass.ds(i * GR + r0 * GR, GR)], dot16).then_inc(dot_saved, 1)
                    dve.wait_ge(dot_saved, i + (SEL // GR * tt + r0 + 1))

            for tt in range(2):
                wait_out(dve, *[f"{nm}{tt}_{m}" for nm in ("xn", "hn") for m in range(2)])
                if tt == 0:
                    for m in range(4):
                        dot_rounds(0, 2 * m, 2)
                        choose(1, m)
                    dve.sem_inc(eidx_ready, 1)
                else:
                    dot_rounds(1, 0, SEL // GR)
                dve.sem_inc(dots_ready, 1)
                share(tt)
                dve.wait_ge(gelu_ready, tt + 1)
                link(v.tensor_tensor(coef[:, tt, :], coef[:, tt, :], gsel[:, tt, :], ALU.mult))
                if tt:
                    dve.wait_ge(out_written, 16 * tt)
                link(v.tensor_copy(yacc, hnat[:, tt, :]))
                first = (2 * tt + 1) * (SEL // GR)
                with dve.Fori(0, SEL // GR, 1) as i:
                    v.tensor_copy(coef16, coef[:, tt, bass.ds(i * GR, GR)]).then_inc(coef_copied, 1)
                    dve.wait_ge(coef_copied, i + (SEL // GR * tt + 1))
                    for j in range(GR):
                        dve.wait_ge(row_loaded[j], i * 16 + 16 * (first + 1))
                        v.scalar_tensor_tensor(yacc, grow(j), coef16[:, j:j + 1], yacc, ALU.mult,
                                               ALU.add).then_inc(rows_free, 1)
                        dve.wait_ge(rows_free, i * GR + (GR * (first + 1) + j + 1))
                dve.sem_inc(y_ready2, 1)
                dve.wait_ge(fsum_ready, 2 * tt + 1)
                link(v.tensor_scalar(fsq[:, 1:2], fsq[:, 0:1], 1.0 / D, EPS, ALU.mult, ALU.add))
                link(v.reciprocal(fsq[:, 1:2], fsq[:, 1:2]))
                dve.sem_inc(y_ready2, 1)
                dve.wait_ge(fsum_ready, 2 * tt + 2)
                dve.wait_ge(gfin_loaded, 16)
                link(v.scalar_tensor_tensor(yacc, yacc, fsq[:, 2:3], gfin, ALU.mult, ALU.mult))
                dve.sem_inc(fin_ready, 1)

        @block.tensor
        def _(pe):
            mm = nc.tensor.matmul

            def open_bank(name):
                _, b, used = plan.at[name]
                if used:
                    pe.wait_ge(bank_free[b], used)
                return bank[b]

            def transposed(dst, src, n):
                return nc.tensor.transpose(dst, src, ident[0:n, 0:n])

            pe.wait_ge(consts_built, 1)
            pe.wait_ge(x_loaded, 32)
            for kt in range(KT):
                pb = open_bank(f"xT{kt}")
                cols = slice(kt * P, (kt + 1) * P)
                transposed(pb[:, 0:META], metanat[0:META, cols], META)
                for tt in range(2):
                    last = transposed(pb[:, META + tt * P:META + (tt + 1) * P], xnat[:, tt, cols], P)
                last.then_inc(group_done, 1)
            pe.wait_ge(rows_loaded, 16 * N_ROW_DMAS)
            pb = open_bank("par")
            transposed(pb[:, 0:15 * KT], rows[0:15 * KT, 0, :], 15 * KT)
            transposed(pb[:, 128:128 + CK * RT], rows[0:CK * RT, 1, :], CK * RT)
            transposed(pb[:, 256:256 + 10 * RT + ZT], rows[0:10 * RT + ZT, 2, :],
                       10 * RT + ZT).then_inc(group_done, 1)

            def norm(j):
                c = norm_cols(j)
                pb = open_bank(f"ms{j}")
                for kt in range(KT):
                    pe.wait_ge(sq_ready, KT * j + kt + 1)
                    last = mm(pb[:, 0:c.stop - c.start], mean_d[:], sq[:, kt, c], start=kt == 0, stop=kt == KT - 1)
                last.then_inc(group_done, 1)

            def slot(s, cols=256):
                pe.wait_ge(w_loaded[s % RING], 16 * (s // RING + 1))
                return wring[:, s % RING, :].rearrange("p (k n) -> p k n", n=cols)

            def project(names, s0, moving, kts, cols=256, ready=None):
                per = cols // P
                for g_, name in enumerate(names):
                    if g_ % per == 0:
                        w = slot(s0 + g_ // per, cols)
                    pb = open_bank(name)
                    for kt in range(kts):
                        if g_ == 0 and ready is not None:
                            pe.wait_ge(*ready(kt))
                        r = moving(kt)
                        last = mm(pb[:, 0:r.shape[-1]], w[:, kt, (g_ % per) * P:(g_ % per + 1) * P], r,
                                  start=kt == 0, stop=kt == kts - 1)
                    last.then_inc(group_done, 1)

            def h_real(kt):
                return hT[:, kt, real]

            def h_all(kt):
                return hT[:, kt, :]

            def h_wait(j):
                return lambda kt: (h_ready, KT * H_AT[j] + kt + 1)

            norm(0)
            project([f"q{m}" for m in range(KT)], SLOTS["qkv"], h_real, KT, ready=h_wait(0))
            project([f"k{m}" for m in range(KT)], SLOTS["qkv"] + 4, h_real, KT)
            for j in range(4):
                w = slot(SLOTS["qkv"] + 8 + j)
                for tt in range(2):
                    pb = open_bank(f"v{j}_{tt}")
                    for kt in range(KT):
                        last = mm(pb[:, 0:256], hT[:, kt, META + tt * P:META + (tt + 1) * P], w[:, kt, :],
                                  start=kt == 0, stop=kt == KT - 1)
                    last.then_inc(group_done, 1)
            wait_out(pe, *[f"{n}{m}" for n in "qk" for m in range(KT)])
            wait_out(pe, *[f"v{j}_{tt}" for j in range(4) for tt in range(2)])
            for i in range(HEADS + 2):
                if i < HEADS:
                    pb = open_bank(f"z{i}")
                    ch = slice(HD * (i % 2), HD * (i % 2 + 1))
                    mm(pb[:, 0:256], kT[ch, i // 2, 0:P], qT[ch, i // 2, :], start=True, stop=True)
                    mm(pb[:, 256:384], kT[ch, i // 2, P:2 * P], qT[ch, i // 2, P:2 * P], start=False, stop=True,
                       skip_group_check=True).then_inc(group_done, 1)
                if 1 <= i <= HEADS:
                    pe.wait_ge(sp_ready, i)
                    pb = bank[plan.at[f"z{i - 1}"][1]]
                    s_ = sp[:, (i - 1) % 2, :]
                    mm(pb[:, 0:256], neg_tri[:], s_[:, 0:256], start=False, stop=True, skip_group_check=True)
                    mm(pb[:, P:256], neg_one[:], s_[:, 256:384], start=False, stop=True, skip_group_check=True)
                    mm(pb[:, 256:384], neg_tri[:], s_[:, 256:384], start=False, stop=True,
                       skip_group_check=True).then_inc(cum_done, 1)
                if i >= 2:
                    h = i - 2
                    if h % 2 == 0:
                        pb = open_bank(f"o{h // 2}")
                    else:
                        pb = bank[plan.at[f"o{h // 2}"][1]]
                    pe.wait_ge(w_ready, h + 1)
                    o_ = pb[HD * (h % 2):HD * (h % 2 + 1), :]
                    mm(o_[:, 0:256], V[:, 0, h * HD:(h + 1) * HD], wexp[:, h % 2, 0:256], start=True, stop=False)
                    last = mm(o_[:, P:256], V[:, 1, h * HD:(h + 1) * HD], wexp[:, h % 2, 256:384],
                              start=False, stop=True)
                    last.then_inc(group_done if h % 2 else o_done, 1)
            wait_out(pe, *[f"o{q}" for q in range(KT)])
            project([f"wo{m}" for m in range(KT)], SLOTS["wo"], lambda kt: oT[:, kt, :], KT)

            def mlp(layer):
                norm(1 + 2 * layer)
                pe.wait_ge(h_ready, KT * (H_AT[1 + 2 * layer] + 1))
                split0 = layer * MLP_UNITS

                def products(bank_, unit, moving, kt, start, stop):
                    high, low = (w[:, unit % UNITS, kt, :] for w in w_hl)
                    mm(bank_, high, moving[0][:, kt, :], start=start, stop=False)
                    mm(bank_, high, moving[1][:, kt, :], start=False, stop=False)
                    return mm(bank_, low, moving[0][:, kt, :], start=False, stop=stop)

                n0, banks, used = plan.at[f"up{layer}"]
                with pe.Fori(0, 4, 1) as i:
                    for j in range(BANKS):
                        pe.wait_ge(w_split, i * 8 + (split0 + j + 1))
                        pe.wait_ge(bank_free[banks[j]], i + used[j])
                        for kt in range(KT):
                            last = products(bank[banks[j]][:, 0:SEQ], j, x_hl, kt, kt == 0, kt == KT - 1)
                        last.then_inc(group_done, 1)
                n0, banks, used = plan.at[f"down{layer}"]
                pe.wait_ge(u_step, 3 * FF // P * (layer + 1))
                with pe.Fori(0, 4, 1) as i:
                    for j in range(2):
                        pe.wait_ge(bank_free[banks[j]], i + used[j])
                    for q in range(4):
                        for j in range(2):
                            pe.wait_ge(w_split, i * 8 + (split0 + MLP_UNITS // 2 + 2 * q + j + 1))
                            u_q = [u_[:, q * KT:(q + 1) * KT, :] for u_ in u_hl]
                            for kt in range(KT):
                                last = products(bank[banks[j]][:, 0:SEQ], 2 * q + j, u_q, kt,
                                                q == 0 and kt == 0, q == 3 and kt == KT - 1)
                            last.then_inc(group_done, 1)

            mlp(0)
            norm(2)
            project([f"rg{m}" for m in range(2 * KT)], SLOTS["rg_in"], h_real, KT, ready=h_wait(2))
            pe.wait_ge(bd_loaded, 64)
            for m in range(KT):
                pe.wait_ge(xc_ready, m + 2)
                pb = open_bank(f"ri{m}")
                mm(pb[:, 0:SEQ], bd[:, 0, m, :], xc[:, m, :], start=True, stop=True)
                mm(pb[:, SEQ:2 * SEQ], bd[:, 1, m, :], xc[:, m, :], start=True, stop=True).then_inc(group_done, 1)
            pe.wait_ge(y_ready, 1)
            project([f"rgo{m}" for m in range(KT)], SLOTS["rg_o"], lambda kt: gate[:, kt, :], KT)
            mlp(1)
            norm(4)
            norm(5)
            project([f"zr{m}" for m in range(ZT)], SLOTS["w_rwkv"], h_all, KT, ready=h_wait(5))
            project([f"{n}{m}" for n in ("val", "cg") for m in range(RT)], SLOTS["w_conv"], h_all, KT)

            def one(name, lhsT, rhs):
                pb = open_bank(name)
                mm(pb[:, 0:rhs.shape[-1]], lhsT, rhs, start=True, stop=True).then_inc(group_done, 1)

            pe.wait_ge(kks_ready, 1)
            for m in range(RT):
                one(f"kks{m}", head_sum[:], Kh[:, m, :])
            pe.wait_ge(updown_loaded, 48)
            pe.wait_ge(lw_ready, 2)
            for m in range(RT):
                one(f"wp{m}", updown[0:64, m * P:(m + 1) * P], tlw[0:64])
            for m in range(RT):
                one(f"ap{m}", updown[64:128, m * P:(m + 1) * P], zf[64:128, 12, :])
            for m in range(RT):
                one(f"gp{m}", gup[:, m * P:(m + 1) * P], slg)
            pe.wait_ge(rk_ready, 1)
            for m in range(RT):
                one(f"bon{m}", head_sum[:], Kh[:, m, CH:WT])
            pe.wait_ge(kb_ready, 1)
            for tt in range(3):
                n = CH if tt == 0 else P
                c0 = 0 if tt == 0 else CH + (tt - 1) * P
                for s_, src in enumerate((vZ, Kh, Bh)):
                    pb = open_bank(f"nat{s_}_{tt}")
                    for m in range(RT):
                        last = transposed(pb[0:n, m * P:(m + 1) * P], src[:, m, c0:c0 + n], P)
                    last.then_inc(group_done, 1)

            def head(t, h, c):
                return t[HD * (h % 2):HD * (h % 2 + 1), h // 2, CH * c:CH * (c + 1)]

            def chunks_of(tt):
                return [0] if tt == 0 else [2 * tt - 1, 2 * tt]

            for tt in range(3):
                for s_, (left, right) in enumerate(((aa, kk), (kk, aa), (kZ, kk), (kZ, rZ), (aa, rZ))[:5 if tt else 3]):
                    for par_ in range(2):
                        pb = open_bank(f"mat{s_}_{par_}_{tt}")
                        for half, c in enumerate(chunks_of(tt)):
                            for q in range(4):
                                last = mm(pb[CH * half:CH * (half + 1), CH * q:CH * (q + 1)],
                                          head(left, 2 * q + par_, c), head(right, 2 * q + par_, c),
                                          start=True, stop=True)
                        last.then_inc(group_done, 1)

            def per_chunk(name, left, right, tt):
                pb = open_bank(name)
                for half in range(len(chunks_of(tt))):
                    r_ = slice(CH * half, CH * (half + 1))
                    for h in range(RH):
                        last = mm(pb[r_, CH * h:CH * (h + 1)], left[r_, tt, h, :], right[r_, tt, h, :],
                                  start=True, stop=True)
                last.then_inc(group_done, 1)

            for lv in range(1, LEVELS):
                for tt in range(3):
                    pe.wait_ge(mt_ready, 3 * (lv - 1) + tt + 1)
                    per_chunk(f"Y{lv}_{tt}", MT, X, tt)
                for tt in range(3):
                    wait_out(pe, f"Y{lv}_{tt}")
                    if lv < LEVELS - 1:
                        per_chunk(f"XY{lv}_{tt}", XT, Y, tt)
                    per_chunk(f"YX{lv}_{tt}", Y, XT, tt)
            natv = nat[0].rearrange("p t (h v) -> p t h v", v=HD)
            wait_out(pe, *[f"mat2_{par_}_{tt}" for tt in range(3) for par_ in range(2)])
            for tt in range(3):
                per_chunk(f"GV_{tt}", G1, natv, tt)
            wait_out(pe, *[f"YX{LEVELS - 1}_{tt}" for tt in range(3)])
            for c in range(NCH):
                tt = (c + 1) // 2
                p0 = CH * ((c - 1) % 2) if c else 0
                r_ = slice(p0, p0 + CH)
                old = ST[:, c % 2]
                if c:
                    pe.wait_ge(st_ready, c)
                    for par_ in range(2):
                        pb = open_bank(f"SA{par_}_{c}")
                        for q in range(4):
                            last = mm(pb[r_, CH * q:CH * (q + 1)], head(kk, 2 * q + par_, c),
                                      old[HD * par_:HD * (par_ + 1), q, :], start=True, stop=True)
                        last.then_inc(group_done, 1)
                pb = open_bank(f"U_{c}")
                pe.wait_ge(yc_ready, c + 1)
                for h in range(RH):
                    last = mm(pb[r_, CH * h:CH * (h + 1)], XT[r_, tt, h, :], Yc[r_, h, :], start=True, stop=True)
                last.then_inc(group_done, 1)
                wait_out(pe, f"U_{c}")
                pb = open_bank(f"S_{c}")
                for h in range(RH):
                    o_ = pb[HD * (h % 2):HD * (h % 2 + 1), CH * (h // 2):CH * (h // 2 + 1)]
                    hc = slice(HD * h, HD * (h + 1))
                    mm(o_, nat[1][r_, tt, hc], nat[0][r_, tt, hc], start=True, stop=False)
                    last = mm(o_, nat[2][r_, tt, hc], Uc[r_, h, :], start=False, stop=True)
                last.then_inc(group_done, 1)
                if c:
                    pb = open_bank(f"OA_{c}")
                    for h in range(RH):
                        h_ = slice(HD * (h % 2), HD * (h % 2 + 1))
                        last = mm(pb[h_, CH * (h // 2):CH * (h // 2 + 1)], old[h_, h // 2, :], head(rZ, h, c),
                                  start=True, stop=True)
                    last.then_inc(group_done, 1)
                    pb = open_bank(f"OB_{c}")
                    for h in range(RH):
                        o_ = pb[HD * (h % 2):HD * (h % 2 + 1), CH * (h // 2):CH * (h // 2 + 1)]
                        mm(o_, nat[0][r_, tt, HD * h:HD * (h + 1)], G2[r_, tt - 1, h, :], start=True, stop=False)
                        last = mm(o_, Uc[r_, h, :], G3[r_, tt - 1, h, :], start=False, stop=True)
                    last.then_inc(group_done, 1)
            pe.wait_ge(owk_ready, 1)
            for m in range(RT):
                one(f"gm{m}", head_mean[:], owk[:, m, :])
            pe.wait_ge(osq_ready, 1)
            for m in range(RT):
                one(f"gv{m}", head_mean[:], osq[:, m, :])
            project([f"gl{m}" for m in range(2 * KT)], SLOTS["w_gate"], h_real, KT)
            pe.wait_ge(cy_ready, 1)
            for name, src, s_, n in (("lm", cy, csq_ready, 1), ("lv", ct, csq_ready, 1)):
                pb = open_bank(name)
                if name == "lv":
                    pe.wait_ge(csq_ready, 1)
                for m in range(RT):
                    last = mm(pb[:, 0:SEQ], mean_c[:], src[:, m, :], start=m == 0, stop=m == RT - 1)
                last.then_inc(group_done, 1)
            pe.wait_ge(yb_in, 1)
            project([f"yb{m}" for m in range(KT)], SLOTS["rwkv_out"], lambda kt: owk[:, kt, :], RT, cols=512)
            pe.wait_ge(cin_sig, 2)
            project([f"ya{m}" for m in range(KT)], SLOTS["conv_out"], lambda kt: cy[:, kt, :], RT, cols=512)
            pe.wait_ge(mix_ready, KT)
            project([f"wo2{m}" for m in range(KT)], SLOTS["wo2"], lambda kt: mix[:, kt, :], KT)
            norm(6)
            w = slot(SLOTS["keys"], NK)
            for m in range(4):
                pb = open_bank(f"key{m}")
                for j in range(4):
                    last = transposed(pb[:, j * P:(j + 1) * P], w[:, 4 * m + j, :], P)
                last.then_inc(group_done, 1)
            wait_out(pe, *[f"key{m}" for m in range(4)])

            def scores(tt, m):
                pb = open_bank(f"sc{tt}_{m}")
                wait_out(pe, *[f"pq{j}" for j in range(4 * m, 4 * m + 4)])
                for j in range(4):
                    last = mm(pb[:, j * P:(j + 1) * P], pq[:, 4 * m + j, tt * P:(tt + 1) * P],
                              keyT[:, 4 * m + j, :], start=True, stop=True)
                last.then_inc(group_done, 1)

            for m in range(5):
                if m < 4:
                    project([f"pq{j}" for j in range(4 * m, 4 * m + 4)], SLOTS["w_q"] + 2 * m, h_real, KT,
                            ready=h_wait(6) if m == 0 else None)
                if m:
                    scores(0, m - 1)
            for tt in range(2):
                for m in range(4 if tt else 0):
                    scores(1, m)
                for name, src in (("xn", hT), ("hn", xT)):
                    for m in range(2):
                        pb = open_bank(f"{name}{tt}_{m}")
                        for j in range(4):
                            last = transposed(pb[:, j * P:(j + 1) * P],
                                              src[:, 4 * m + j, META + tt * P:META + (tt + 1) * P], P)
                        last.then_inc(group_done, 1)


_INS = ['x', 'norm_mix', 'norm_mlp', 'mlp_w1', 'mlp_w2', 'sb_w_qkv', 'sb_w_o', 'rg_w_in', 'rg_conv_w',
        'rg_conv_b', 'rg_w_a', 'rg_b_a', 'rg_w_x', 'rg_b_x', 'rg_lambda', 'rg_w_o', 'norm_final',
        'meta_tokens_2', 'g_mix_2', 'w_in_2', 'conv_w_2', 'conv_b_2', 'conv_ln_g_2', 'conv_ln_b_2',
        'w_conv_out_2', 'mu_shift_2', 'w0_2', 'w_up_2', 'a0_2', 'a_up_2', 'g_up_2', 'k_k_2', 'k_a_2',
        'r_k_2', 'gn_g_2', 'gn_b_2', 'w_rwkv_out_2', 'w_o_2', 'g_ffn_2', 'w_q_2', 'sub_keys_2',
        'expert_u_2', 'expert_v_2', 'g_final_2']


def kernel(**inputs):
    import numpy as _np
    import concourse.bacc as _bacc
    from concourse import mybir as _mybir
    from concourse.bass_utils import run_bass_kernel_spmd as _run

    nc = _bacc.Bacc("TRN2", target_bir_lowering=False, num_devices=1)
    arrays, args = {}, []
    for name in _INS:
        a = _np.ascontiguousarray(inputs[name])
        arrays[f"in_{name}_dram"] = a
        args.append(nc.dram_tensor(f"in_{name}_dram", a.shape, _mybir.dt.from_np(a.dtype), kind="ExternalInput").ap())
    shape = (1, SEQ, D)
    args.append(nc.dram_tensor("out_0_dram", shape, _mybir.dt.float32, kind="ExternalOutput").ap())
    build(nc, *args)
    r = _run(nc, [arrays], core_ids=[0])
    return r.results[0]["out_0_dram"]
```

```python
import math
import concourse.bass as bass
from concourse import mybir
from contextlib import ExitStack

F32 = mybir.dt.float32
F32R = mybir.dt.float32r
U32 = mybir.dt.uint32
ALU = mybir.AluOpType
ACT = mybir.ActivationFunctionType
AX = mybir.AxisListType

P = 128
D = 1024
KT = D // P
SEQ = 256
META = 16
TOK = META + SEQ
FF = 4 * D
HEADS = 16
HD = 64
CONV = 4
CK = 31
RW = 512
RT = RW // P
RH = RW // HD
CH = 64
NCH = 5
WT = NCH * CH
PADC = CH - META
ZT = 14
PH = 8
NK = 128
TOPK = 16
SEL = PH * TOPK
EPS, LN_EPS, GN_EPS = 1e-6, 1e-5, 64e-5
DECAY = -math.exp(-0.5)
LEVELS = 6

RING = 4
SLOT = 2048
BANKS = 8
PE_ROWS = (0, 3, 6, 8, 11, 14)
GR = 16
UNITS = 4
MLP_UNITS = 2 * 2 * FF // 256
NEG = -3.0e38
N_ROW_DMAS = 27


class Plan:

    def __init__(self):
        self.n, self.at, self.uses = 0, {}, [0] * BANKS

    def add(self, name, bank=None):
        b = self.n % BANKS if bank is None else bank
        self.n += 1
        self.at[name] = (self.n, b, self.uses[b])
        self.uses[b] += 1

    def loop(self, name, rounds, banks, more=0):
        self.at[name] = (self.n, list(banks), [self.uses[b] for b in banks])
        self.n += rounds * len(banks) * (1 + more)
        for b in banks:
            self.uses[b] += rounds


def make_plan():
    plan = Plan()
    for kt in range(KT):
        plan.add(f"xT{kt}")
    plan.add("par")
    plan.add("ms0")
    for m in range(KT):
        plan.add(f"q{m}")
    for m in range(KT):
        plan.add(f"k{m}")
    for j in range(4):
        for tt in range(2):
            plan.add(f"v{j}_{tt}")
    for i in range(HEADS + 2):
        if i < HEADS:
            plan.add(f"z{i}", i % 3)
        if i >= 2 and i % 2 == 1:
            plan.add(f"o{(i - 2) // 2}", 4 + ((i - 2) // 2) % 2)
    for m in range(KT):
        plan.add(f"wo{m}")
    for layer in range(2):
        if layer == 1:
            plan.add("ms2")
            for m in range(2 * KT):
                plan.add(f"rg{m}")
            for m in range(KT):
                plan.add(f"ri{m}")
            for m in range(KT):
                plan.add(f"rgo{m}")
        plan.add(f"ms{1 + 2 * layer}")
        plan.loop(f"up{layer}", 4, range(BANKS))
        plan.loop(f"down{layer}", 2, (0, 1, 2, 3), more=3)
    plan.add("ms4")
    plan.add("ms5")
    for m in range(ZT):
        plan.add(f"zr{m}")
    for m in range(RT):
        plan.add(f"kks{m}")
    for m in range(RT):
        plan.add(f"wp{m}")
    for m in range(RT):
        plan.add(f"ap{m}")
    for m in range(RT):
        plan.add(f"gp{m}")
    for m in range(RT):
        plan.add(f"val{m}")
    for m in range(RT):
        plan.add(f"cg{m}")
    for m in range(RT):
        plan.add(f"bon{m}")
    for tt in range(3):
        for s in range(3):
            plan.add(f"nat{s}_{tt}")
    for tt in range(3):
        for s in range(5 if tt else 3):
            for par in range(2):
                plan.add(f"mat{s}_{par}_{tt}")
    for lv in range(1, LEVELS):
        for tt in range(3):
            plan.add(f"Y{lv}_{tt}")
        for tt in range(3):
            if lv < LEVELS - 1:
                plan.add(f"XY{lv}_{tt}")
            plan.add(f"YX{lv}_{tt}")
    for tt in range(3):
        plan.add(f"GV_{tt}")
    for c in range(NCH):
        if c:
            plan.add(f"SA0_{c}")
            plan.add(f"SA1_{c}")
            plan.add(f"OA_{c}")
        plan.add(f"U_{c}")
        plan.add(f"S_{c}")
        if c:
            plan.add(f"OB_{c}")
    for m in range(RT):
        plan.add(f"gm{m}")
    for m in range(RT):
        plan.add(f"gv{m}")
    plan.add("lm")
    for m in range(KT):
        plan.add(f"gl{m}")
    plan.add("lv")
    for m in range(KT, 2 * KT):
        plan.add(f"gl{m}")
    for m in range(KT):
        plan.add(f"yb{m}")
    for m in range(KT):
        plan.add(f"ya{m}")
    for m in range(KT):
        plan.add(f"wo2{m}")
    plan.add("ms6")
    for m in range(4):
        plan.add(f"key{m}")
    for m in range(5):
        for j in range(4 * m, min(4 * m + 4, 2 * PH)):
            plan.add(f"pq{j}")
        if m:
            plan.add(f"sc0_{m - 1}")
    by_act = [plan.at[f"pq{j}"][1] for j in range(2 * PH - 4, 2 * PH)]
    for tt in range(2):
        for j, name in enumerate(("xn", "hn")):
            for m in range(2):
                plan.add(f"{name}{tt}_{m}", by_act[2 * j + m])
    for m, b in enumerate(b for b in range(BANKS) if b not in by_act):
        plan.add(f"sc1_{m}", b)
    return plan


SLOTS = {}
_at = 0
for _name, _count in (("qkv", 12), ("wo", 4), ("up0", 16), ("down0", 16), ("rg_in", 8), ("rg_o", 4),
                      ("up1", 16), ("down1", 16), ("w_rwkv", 7), ("w_conv", 4), ("w_gate", 8),
                      ("rwkv_out", 2), ("conv_out", 2), ("wo2", 4), ("keys", 1), ("w_q", 8)):
    SLOTS[_name] = _at
    _at += _count
N_SLOTS = _at

RS_AT = {0: 1, 1: 2, 2: 3, 3: 4, 4: 5, 5: 6, "gn": 7, "ln": 8, 6: 9}
H_AT = {0: 0, 1: 1, 2: 2, 3: 3, 5: 4, 6: 5}


UNIT = {}
UNITS_OF = []
for _name, _s in SLOTS.items():
    _end = min([_t for _t in SLOTS.values() if _t > _s], default=N_SLOTS)
    UNIT[_name] = len(UNITS_OF)
    for _j in range(_s, _end if _name != "keys" else _s):
        _kind = "wide" if _name in ("rwkv_out", "conv_out") else "rows" if _name == "qkv" and _j >= 8 else "columns"
        UNITS_OF += [(_j, 0, _kind), (_j, 1, _kind)]
N_UNITS = len(UNITS_OF)
assert all(UNIT[f"up{_l}"] % 8 == 0 and SLOTS[f"up{_l}"] % RING == 0 for _l in range(2))


def make_used_at(plan):
    used = [0] * N_UNITS

    def of(phase, *last_groups):
        for j, name in enumerate(last_groups):
            used[UNIT[phase] + j] = plan.at[name][0]

    of("qkv", *[f"{n}{m}" for n in "qk" for m in range(KT)], *[f"v{j // 2}_1" for j in range(8)])
    of("wo", *[f"wo{m}" for m in range(KT)])
    of("rg_in", *[f"rg{m}" for m in range(2 * KT)])
    of("rg_o", *[f"rgo{m}" for m in range(KT)])
    of("w_rwkv", *[f"zr{m}" for m in range(ZT)])
    of("w_conv", *[f"{n}{m}" for n in ("val", "cg") for m in range(RT)])
    of("w_gate", *[f"gl{m}" for m in range(2 * KT)])
    of("rwkv_out", *[f"yb{m}" for m in range(1, KT, 2)])
    of("conv_out", *[f"ya{m}" for m in range(1, KT, 2)])
    of("wo2", *[f"wo2{m}" for m in range(KT)])
    of("w_q", *[f"pq{m}" for m in range(2 * PH)])
    for layer in range(2):
        for j in range(MLP_UNITS):
            used[UNIT[f"up{layer}"] + j] = plan.at[f"up{layer}"][0] + j + 1
    assert all(used)
    return used


def make_release(plan):
    rel = {SLOTS["keys"]: (False, plan.at["key3"][0])}
    for n, (s, _, _) in enumerate(UNITS_OF):
        rel[s] = (True, n + 1)
    return rel



def build(nc, x, norm_mix, norm_mlp, mlp_w1, mlp_w2, sb_w_qkv, sb_w_o, rg_w_in, rg_conv_w,
          rg_conv_b, rg_w_a, rg_b_a, rg_w_x, rg_b_x, rg_lambda, rg_w_o, norm_final, meta_tokens,
          g_mix, w_in, conv_w, conv_b, conv_ln_g, conv_ln_b, w_conv_out, mu_shift, w0, w_up, a0,
          a_up, g_up, k_k, k_a, r_k, gn_g, gn_b, w_rwkv_out, w_o2, g_ffn, w_q, sub_keys, expert_u,
          expert_v, g_final, out):
    ctx = ExitStack()
    with ctx:
        def sb(name, shape, dt=F32):
            return ctx.enter_context(nc.sbuf_tensor(name, shape, dt))

        def sem(name):
            return ctx.enter_context(nc.semaphore(name))

        plan = make_plan()
        release = make_release(plan)
        used_at = make_used_at(plan)
        bank = [ctx.enter_context(nc.psum_tensor(f"bank{b}", [P, 512], F32)) for b in range(BANKS)]

        wring = sb("wring", [P, RING, SLOT])
        xT = sb("xT", [P, KT, TOK])
        sq = sb("sq", [P, KT, TOK])
        hT = sq
        h_hl = [sb(f"h_{part}", [P, KT, TOK], F32R) for part in ("high", "low")]
        rs = sb("rs", [P, WT])
        rtmp = sb("rtmp", [P, WT])
        par = sb("par", [P, 320])
        ident = sb("ident", [P, P])
        mean_d = sb("mean_d", [P, P])
        mean_c = sb("mean_c", [P, P])
        head_sum = sb("head_sum", [P, P])
        head_mean = sb("head_mean", [P, P])
        neg_tri = sb("neg_tri", [P, P])
        neg_one = sb("neg_one", [P, P])
        attn_mask = sb("attn_mask", [P, 3 * P])
        strict = sb("strict", [P, CH])
        lower = sb("lower", [P, CH])
        incl = sb("incl", [P, CH])
        nincl = sb("nincl", [P, CH])
        eye = sb("eye", [P, CH])
        lvl = sb("lvl", [P, 2 * LEVELS, CH])
        reset = sb("reset", [P, WT])
        updown = sb("updown", [P, RW])
        gup = sb("gup", [P, RW])
        lamc = sb("lamc", [P, 5, KT])
        omka = sb("omka", [P, RT])
        pend = sb("pend", [P, RT, NCH])
        SPLIT_C, SPLIT_D = 17568, 6840

        def overlay(*tensors):
            made, at = [], 0
            with ExitStack() as stack:
                for t in tensors:
                    if isinstance(t, int):
                        stack.enter_context(nc.sbuf_tensor(f"gap{at}_{t}", [P, t - at], F32))
                        at = t
                        continue
                    name, *shape = t
                    made.append([stack.enter_context(nc.sbuf_tensor(f"{name}_{part}", [P, *shape], F32R))
                                 for part in ("high", "low")])
                    at += 2 * math.prod(shape)
            return made, at

        (w_a, m_hl), _ = overlay(("w_a", UNITS, KT * P), 10240, ("m", KT, SEQ))
        (u_hl,), SPLIT_END = overlay(2 * UNITS * KT * P, ("u", FF // P, SEQ))
        (y_hl, w_d, w_c), _ = overlay(("y", 2 * RT, SEQ), SPLIT_D, ("w_d", UNITS, KT * P), SPLIT_C,
                                      ("w_c", UNITS, KT * P))
        ARENA = 27942
        arena = sb("arena", [P, ARENA])

        def area(at, *shape):
            size = math.prod(shape)
            assert at + size <= ARENA, (at, shape)
            flat = arena[:, at:at + size]
            if len(shape) == 1:
                return flat
            if len(shape) == 2:
                return flat.rearrange("p (a b) -> p a b", b=shape[1])
            return flat.rearrange("p (a b c) -> p a b c", b=shape[1], c=shape[2])

        xnat, metanat, rows = area(8192, 2, D), area(10240, D), area(11264, 3, P)
        qT, kT, V = area(14336, KT, SEQ), area(16384, KT, SEQ), area(18432, 2, D)
        lnz, sp, wexp = area(20480, 2, 384), area(21248, 2, 384), area(22016, 2, 384)
        mtmp = area(22784, P)
        utmp = area(SPLIT_END, 4, SEQ)
        xg = area(20480, KT, SEQ)
        gate = area(8192, KT, SEQ)
        xraw = area(10240, KT, SEQ + CONV - 1)
        xc = area(12312, KT, SEQ)
        rS, iS, aS, tS, mS = (area(14360 + 2048 * j, KT, SEQ) for j in range(5))
        bd = area(24600, 2, KT, P)
        U, gg, bonus = area(0, RT, CK - 1 + TOK), area(1208, RT, SEQ), area(2232, RT, SEQ)
        zf = area(3256, ZT, WT)
        rZ, kZ, vZ = zf[:, 0:RT, :], zf[:, RT:2 * RT, :], zf[:, 2 * RT:3 * RT, :]
        kk, aa = area(7736, RT, WT), area(9016, RT, WT)
        zr = area(10296, ZT, TOK + 1)
        ld, LP, Pd, Kh, Bh = (area(10296 + 1280 * j, RT, WT) for j in range(5))
        Pi = LP
        tlw, slg = area(16696, WT), area(17016, SEQ)
        val, cg = area(25766, RT, TOK), area(26854, RT, TOK)
        Nm, NT, X, XT, Y, MT = (area(10296 + 1536 * j, 3, RH, CH) for j in range(6))
        nat = [area(21798 + 1536 * j, 3, RW) for j in range(3)]
        G1, G2, G3 = area(26406, 3, RH, CH), area(19512, 2, RH, CH), area(20536, 2, RH, CH)
        owk, Yc, Uc, ST = area(16440, RT, SEQ), area(17464, RH, CH), area(17976, RH, CH), area(18488, 2, RT, CH)
        cy = area(5816, RT, SEQ)
        GAB = area(21798, 2 * KT, SEQ)
        mix, mt2, ct = area(17464, KT, SEQ), area(19512, SEQ), area(19768, RT, SEQ)
        osq, orr = area(25894, RT, SEQ), area(26918, RT, SEQ)
        keyT, pq = area(0, 2 * PH, NK), area(2048, 2 * PH, SEQ)
        hnat, fnat = area(6840, 2, D), area(8888, 2, D)
        g_arena = area(10936, 4, D)
        sc, sc2 = area(15032, 2 * PH, NK), area(17080, 2 * PH, NK)
        cand, cand2 = area(19128, PH, TOPK * TOPK), area(21176, PH, TOPK * TOPK)
        oh = cand2.rearrange("p h n -> p (h n)").rearrange("p (s k) -> p s k", k=TOPK)
        topv, topf = area(23224, 2 * PH, TOPK), area(23480, 2 * PH, TOPK)
        bv, rowf, colf, i1f, i2f = (area(23736 + 128 * j, PH, TOPK) for j in range(5))
        psm = area(24376, PH)
        gsel, dots, coef = (area(24388 + 256 * j, 2, SEL) for j in range(3))
        dot16 = area(25156, GR)
        coef16 = area(25172, GR)
        fsq = area(25188, 4)
        junk = area(25192, D)
        yacc = area(26216, D)
        gfin = area(17080, D)
        diag = area(2048, len(PE_ROWS), P)
        y_banks = [[bank[plan.at[f"{name}1_{m}"][1]] for m in range(2)] for name in ("xn", "hn")]
        io16 = sb("io16", [P, TOPK])
        topi = sb("topi", [P, 2 * PH, TOPK], U32)
        bi = sb("bi", [P, PH, TOPK], U32)
        bt, bt2 = sb("bt", [P, PH, TOPK], U32), sb("bt2", [P, PH, TOPK], U32)
        eidx = sb("eidx", [P, 2, SEL], U32)
        eix = [sb(f"eix{h}", [P, GR], U32) for h in range(2)]

        def grow(j):
            if j < 8:
                return wring[:, j // 2, (j % 2) * D:(j % 2 + 1) * D]
            if j < 12:
                return g_arena[:, j - 8, :]
            t = (sq if j < 14 else xT)[:].rearrange("p k n -> p (k n)")
            return t[:, (j % 2) * D:(j % 2 + 1) * D]

        consts_built, pool_chain, act_chain, dve_chain = map(sem, (
            "consts_built", "pool_chain", "act_chain", "dve_chain"))
        x_loaded, rows_loaded, bd_loaded, updown_loaded, gfin_loaded = map(sem, (
            "x_loaded", "rows_loaded", "bd_loaded", "updown_loaded", "gfin_loaded"))
        w_loaded = [sem(f"w_loaded{j}") for j in range(RING)]
        group_done = sem("group_done")
        bank_free = [sem(f"bank_free{b}") for b in range(BANKS)]
        x_ready, sq_ready, mean_ready, rs_ready, h_ready = map(sem, (
            "x_ready", "sq_ready", "mean_ready", "rs_ready", "h_ready"))
        lnz_ready, sp_ready, cum_done, w_ready, o_done, u_step = map(sem, (
            "lnz_ready", "sp_ready", "cum_done", "w_ready", "o_done", "u_step"))
        h_whole, h_high, w_high, w_split, gate_high, y_high, y_split, mix_high = map(sem, (
            "h_whole", "h_high", "w_high", "w_split", "gate_high", "y_high", "y_split", "mix_high"))
        mix_split = sem("mix_split")
        lam_ready, xc_ready, ri_ready, at_ready, m_ready, mroot_ready, y_ready = map(sem, (
            "lam_ready", "xc_ready", "ri_ready", "at_ready", "m_ready", "mroot_ready", "y_ready"))
        zf_ready, kks_ready, lw_ready, kkn_ready, ksq_ready, lp_ready, p_ready, rk_ready, kb_ready = map(sem, (
            "zf_ready", "kks_ready", "lw_ready", "kkn_ready", "ksq_ready", "lp_ready", "p_ready",
            "rk_ready", "kb_ready"))
        mt_ready, yc_ready, st_ready, owk_ready, osq_ready = map(sem, (
            "mt_ready", "yc_ready", "st_ready", "owk_ready", "osq_ready"))
        cy_ready, csq_ready, cin_ready, cin_sig, yb_in, mix_ready = map(sem, (
            "cy_ready", "csq_ready", "cin_ready", "cin_sig", "yb_in", "mix_ready"))
        io_ready, eidx_ready, gsel_ready, gsel_exp = map(sem, (
            "io_ready", "eidx_ready", "gsel_ready", "gsel_exp"))
        row_loaded = [sem(f"row_loaded{j}") for j in range(GR)]
        rows_free, eix_copied, slot_seen, dot_saved, coef_copied, dots_ready, gelu_ready = map(sem, (
            "rows_free", "eix_copied", "slot_seen", "dot_saved", "coef_copied", "dots_ready", "gelu_ready"))
        diag_ready, pe_used, y_step = map(sem, ("diag_ready", "pe_used", "y_step"))
        y_ready2, fsum_ready, fin_ready, out_written = map(sem, (
            "y_ready2", "fsum_ready", "fin_ready", "out_written"))

        def norm_cols(j):
            return slice(0, TOK) if j == 5 else slice(META, TOK)

        real = slice(META, TOK)
        block = ctx.enter_context(nc.Block())

        def wait_group(eng, name):
            n, b, _ = plan.at[name]
            eng.wait_ge(group_done, n)
            return bank[b]

        def free(name):
            return bank_free[plan.at[name][1]]

        def wait_out(eng, *names):
            for name in names:
                _, b, used = plan.at[name]
                eng.wait_ge(bank_free[b], used + 1)

        def raw_unit(n):
            s, half, kind = UNITS_OF[n]
            w = wring[:, s % RING, :].rearrange("p (k n) -> p k n", n=512 if kind == "wide" else 256)
            if kind == "rows":
                return w[:, 4 * half:4 * half + 4, :]
            n = 256 if kind == "wide" else P
            return w[:, :, n * half:n * (half + 1)]

        def unit(n, part):
            w = w_a if n < UNIT["w_rwkv"] else w_c if n < UNIT["w_gate"] else w_d
            return w[part][:, n % UNITS, :].rearrange("p (k n) -> p k n", n=P if UNITS_OF[n][2] == "columns" else 256)

        @block.sync
        def _(sp_):
            def load(s, src, kt, cols):
                if s >= RING:
                    is_split, n = release[s - RING]
                    sp_.wait_ge(w_split if is_split else group_done, n)
                dst = wring[:, s % RING, 0:kt * cols].rearrange("p (k n) -> p k n", n=cols)
                sp_.dma_start(dst, src).then_inc(w_loaded[s % RING], 16)

            def load_columns(name, w, c0, count):
                for j in range(count):
                    load(SLOTS[name] + j,
                         w.rearrange("(k p) n -> p k n", p=P)[:, :, c0 + 256 * j:c0 + 256 * (j + 1)], KT, 256)

            def load_mlp(layer):
                s0, n0 = SLOTS[f"up{layer}"], UNIT[f"up{layer}"]
                up = mlp_w1[layer].rearrange("(k p) (r n) -> p k r n", p=P, n=256)
                down = mlp_w2[layer].rearrange("(q k p) (r n) -> q p k r n", p=P, k=KT, n=256)
                for j in range(RING):
                    load(s0 + j, up[:, :, j, :], KT, 256)
                with sp_.Fori(0, 3, 1) as i:
                    for j in range(RING):
                        sp_.wait_ge(w_split, i * (2 * RING) + (n0 + 2 * (j + 1)))
                        sp_.dma_start(wring[:, (s0 + j) % RING, :].rearrange("p (k n) -> p k n", n=256),
                                      up[:, :, bass.ds(i * RING + (RING + j), 1), :].rearrange("p k r n -> p k (r n)")
                                      ).then_inc(w_loaded[(s0 + j) % RING], 16)
                with sp_.Fori(0, 4, 1) as i:
                    for j in range(RING):
                        sp_.wait_ge(w_split, i * (2 * RING) + (n0 + 3 * 2 * RING + 2 * (j + 1)))
                        sp_.dma_start(wring[:, (s0 + j) % RING, :].rearrange("p (k n) -> p k n", n=256),
                                      down[j][:, :, i, :]).then_inc(w_loaded[(s0 + j) % RING], 16)

            sp_.dma_start(xnat, x[0].rearrange("(t p) n -> p t n", p=P)).then_inc(x_loaded, 16)
            sp_.dma_start(metanat[0:META, :], meta_tokens).then_inc(x_loaded, 16)
            load_columns("qkv", sb_w_qkv[0], 0, 12)
            load_columns("wo", sb_w_o[0], 0, 4)
            load_mlp(0)
            for j in range(8):
                c0 = (D if j < 4 else 0) + 256 * (j % 4)
                load(SLOTS["rg_in"] + j, rg_w_in[0].rearrange("(k p) n -> p k n", p=P)[:, :, c0:c0 + 256], KT, 256)
            load_columns("rg_o", rg_w_o[0], 0, 4)
            load_mlp(1)
            load_columns("w_rwkv", w_in[0], 1024, 7)
            load_columns("w_conv", w_in[0], 0, 4)
            load_columns("w_gate", w_in[0], 1024 + 1792, 8)
            for name, w in (("rwkv_out", w_rwkv_out), ("conv_out", w_conv_out)):
                for j in range(2):
                    load(SLOTS[name] + j,
                         w[0].rearrange("(k p) n -> p k n", p=P)[:, :, 512 * j:512 * (j + 1)], RT, 512)
            load_columns("wo2", w_o2[0], 0, 4)
            load(SLOTS["keys"], sub_keys[0].rearrange("h c n d -> n (h c) d"), 2 * PH, NK)
            load_columns("w_q", w_q[0], 0, 8)
            for tt in range(2):
                sp_.wait_ge(fin_ready, tt + 1)
                sp_.dma_start(out[0, tt * P:(tt + 1) * P, :], yacc).then_inc(out_written, 16)
            sp_.wait_ge(out_written, 32)

        @block.gpsimd
        def _(pool):
            chain = [0]

            def link(ins):
                chain[0] += 1
                ins.then_inc(pool_chain, 1)
                pool.wait_ge(pool_chain, chain[0])

            g = nc.gpsimd

            def keep(t, pattern, base, mult, fill=0.0):
                link(g.affine_select(out=t, in_=t, compare_op=ALU.is_ge, fill=fill, base=base,
                                     pattern=pattern, channel_multiplier=mult))

            link(g.memset(ident[:], 0.0))
            link(g.affine_select(out=ident[:], in_=ident[:], compare_op=ALU.not_equal, fill=1.0, base=0,
                                 pattern=[[-1, P]], channel_multiplier=1))
            g.memset(mean_d[:], 1.0 / D).then_inc(consts_built, 1)
            link(g.memset(neg_one[:], -1.0))
            link(g.memset(neg_tri[:], -1.0))
            keep(neg_tri[:], [[-1, P]], 0, 1)
            link(g.memset(attn_mask[:], 1.0))
            for c in (0, 2):
                keep(attn_mask[:, c * P:(c + 1) * P], [[1, P]], -1, -1)
            pool.sem_inc(consts_built, 1)
            pool.dma_start(updown[0:64, :], w_up[0]).then_inc(updown_loaded, 16)
            pool.dma_start(updown[64:128, :], a_up[0]).then_inc(updown_loaded, 16)
            pool.dma_start(gup[:], g_up[0]).then_inc(updown_loaded, 16)

            def split_low(first, count):
                for n in range(first, first + count):
                    pool.wait_ge(w_high, n + 1)
                    g.tensor_tensor(unit(n, 1), raw_unit(n), unit(n, 0).bitcast(F32),
                                    ALU.subtract).then_inc(w_split, 1)

            def split_low_mlp(layer):
                n0 = UNIT[f"up{layer}"]
                with pool.Fori(0, MLP_UNITS // 8, 1) as i:
                    for j in range(8):
                        pool.wait_ge(w_high, i * 8 + (n0 + j + 1))
                        g.tensor_tensor(unit(n0 + j, 1), raw_unit(n0 + j), unit(n0 + j, 0).bitcast(F32),
                                        ALU.subtract).then_inc(w_split, 1)

            split_low(UNIT["qkv"], UNIT["wo"] + UNITS)
            link(g.memset(mean_c[:], 1.0 / RW))
            link(g.memset(head_sum[:], 1.0))
            hs = head_sum[:].rearrange("p (b j) -> p b j", j=HD)
            keep(hs, [[-HD, 2], [0, HD]], 0, 1)
            keep(hs, [[HD, 2], [0, HD]], HD - 1, -1)
            link(g.tensor_scalar(head_mean[:], head_sum[:], 1.0 / HD, None, ALU.mult))

            def diagonal(dst, make):
                make()
                link(g.tensor_copy(dst[0:CH], mtmp[0:CH, 0:CH]))
                link(g.tensor_copy(dst[CH:P], mtmp[CH:P, CH:P]))

            def tri(step, base, mult):
                def make():
                    link(g.memset(mtmp, 1.0))
                    keep(mtmp, [[step, P]], base, mult)
                return make

            diagonal(strict[:], tri(1, -1, -1))
            diagonal(lower[:], tri(-1, -1, 1))
            diagonal(incl[:], tri(1, 0, -1))
            link(g.tensor_scalar(nincl[:], incl[:], -1.0, None, ALU.mult))
            link(g.tensor_copy(eye[0:CH], ident[0:CH, 0:CH]))
            link(g.tensor_copy(eye[CH:P], ident[CH:P, CH:P]))
            for lv in range(LEVELS):
                b = 1 << lv
                nb = P // (2 * b)

                def block_ts():
                    link(g.memset(mtmp, 1.0))
                    m4 = mtmp.rearrange("p (m h j) -> p m h j", h=2, j=b)
                    keep(m4, [[-2 * b, nb], [-P, 2], [0, b]], -b, 1)
                    keep(m4, [[2 * b, nb], [0, 2], [0, b]], 2 * b - 1, -1)

                def block_st():
                    link(g.memset(mtmp, 1.0))
                    m4 = mtmp.rearrange("p (m h j) -> p m h j", h=2, j=b)
                    keep(m4, [[-2 * b, nb], [P, 2], [0, b]], -P, 1)
                    keep(m4, [[2 * b, nb], [0, 2], [0, b]], b - 1, -1)

                diagonal(lvl[:, lv, :], block_ts)
                diagonal(lvl[:, LEVELS + lv, :], block_st)
            link(g.memset(reset[:], 1.0))
            link(g.memset(reset[:].rearrange("p (c j) -> p c j", j=CH)[:, :, 0:1], 0.0))
            g.iota(io16[:], [[1, TOPK]], base=0, channel_multiplier=0,
                   allow_small_or_imprecise_dtypes=True).then_inc(io_ready, 1)
            pool.sem_inc(consts_built, 1)
            split_low(UNIT["wo"] + UNITS, KT - UNITS)
            split_low_mlp(0)
            split_low(UNIT["rg_in"], UNITS + 1)
            link(g.memset(bd, 0.0))
            for s_, w in ((0, rg_w_a), (1, rg_w_x)):
                wv = w[0].rearrange("(k two) i j -> two i k j", two=2)
                for half in range(2):
                    pool.dma_start(bd[half * HD:(half + 1) * HD, s_, :, half * HD:(half + 1) * HD],
                                   wv[half]).then_inc(bd_loaded, 16)
            split_low(UNIT["rg_in"] + UNITS + 1, 3 * KT - UNITS - 1)
            split_low_mlp(1)
            split_low(UNIT["w_rwkv"], N_UNITS - UNIT["w_rwkv"])
            for tt in range(2):
                for which, table in ((0, expert_u), (1, expert_v)):
                    first = (2 * tt + which) * (SEL // GR)
                    if which == 0 and tt == 0:
                        pool.wait_ge(group_done, plan.at["hn1_1"][0])
                    with pool.Fori(0, SEL // GR // 2, 1) as i:
                        if which == 0:
                            pool.wait_ge(eidx_ready, i + (4 * tt + 1))
                            pool.sem_inc(slot_seen, 1)
                        for half in range(2):
                            r16 = i * (2 * GR) + (first + half) * GR
                            pool.wait_ge(rows_free, r16 + 1)
                            pool.sem_inc(slot_seen, 1)
                            g.tensor_copy(eix[half][:], eidx[:, tt, bass.ds(i * (2 * GR) + half * GR, GR)]
                                          ).then_inc(eix_copied, 1)
                            pool.wait_ge(eix_copied, i * 2 + (first + half + 1))
                            for j in range(GR):
                                pool.wait_ge(rows_free, r16 + (j + 1))
                                pool.sem_inc(slot_seen, 1)
                                g.indirect_dma_start(
                                    out=grow(j), out_offset=None, in_=table[0],
                                    in_offset=bass.IndirectOffsetOnAxis(ap=eix[half][:, j:j + 1], axis=0)
                                ).then_inc(row_loaded[j], 16)

        @block.scalar
        def _(act):
            chain = [0]
            a = nc.scalar

            def link(ins):
                chain[0] += 1
                ins.then_inc(act_chain, 1)
                act.wait_ge(act_chain, chain[0])


            def row(t, at, v, r):
                act.dma_start(rows[at:at + r, t, :], v.rearrange("(r p) -> r p", p=P)).then_inc(rows_loaded, 16)

            for v, src in enumerate((norm_mix[0], norm_mix[1], norm_mlp[0], norm_mlp[1], norm_final)):
                row(0, v * KT, src, KT)
            for v in range(CONV):
                row(0, (5 + v) * KT, rg_conv_w[0, v], KT)
            for v, src in enumerate((rg_conv_b[0], rg_b_a[0], rg_b_x[0], rg_lambda[0], g_mix[0], g_ffn[0])):
                row(0, (9 + v) * KT, src, KT)
            act.dma_start(rows[0:CK * RT, 1, :],
                          conv_w[0].rearrange("t (r p) -> (t r) p", p=P)).then_inc(rows_loaded, 16)
            for v, src in enumerate((conv_b[0], conv_ln_g[0], conv_ln_b[0], w0[0], a0[0], k_k[0], k_a[0],
                                     r_k[0].rearrange("h n -> (h n)"), gn_g[0], gn_b[0])):
                row(2, v * RT, src, RT)
            row(2, 10 * RT, mu_shift[0], ZT)

            split = [0]

            def split_high(count=1):
                for n in range(split[0], split[0] + count):
                    s = UNITS_OF[n][0]
                    act.wait_ge(w_loaded[s % RING], 16 * (s // RING + 1))
                    if n >= UNITS and n not in (range(UNIT["w_gate"], UNIT["w_gate"] + UNITS)):
                        act.wait_ge(group_done, used_at[n - UNITS])
                    a.activation(unit(n, 0), raw_unit(n), ACT.Copy).then_inc(w_high, 1)
                split[0] += count

            def split_mlp(layer):
                n0 = UNIT[f"up{layer}"]
                with act.Fori(0, MLP_UNITS // 8 - 1, 1) as i:
                    for n in range(n0 + UNITS, n0 + UNITS + 8):
                        s = UNITS_OF[n][0]
                        act.wait_ge(w_loaded[s % RING], i * 16 + 16 * (s // RING + 1))
                        act.wait_ge(group_done, i * 8 + used_at[n - UNITS])
                        a.activation(unit(n0 + n % 8, 0), raw_unit(n), ACT.Copy).then_inc(w_high, 1)
                split[0] += MLP_UNITS - 8
                split_high(UNITS)

            def norm(j, whole=0, units=False, after=0):
                c = norm_cols(j)

                def high(kt):
                    act.wait_ge(h_whole, KT * H_AT[j] + kt + 1)
                    a.activation(h_hl[0][:, kt, c], xg[:, kt, :] if whole == 1 else hT[:, kt, c],
                                 ACT.Copy).then_inc(h_high, 1)

                for kt in range(KT):
                    if units:
                        split_high()
                    act.wait_ge(x_ready, KT * j + kt + 1)
                    a.activation(sq[:, kt, c], xT[:, kt, c], ACT.Square).then_inc(sq_ready, 1)
                    if whole == 1:
                        high(kt)
                split_high(after)
                act.wait_ge(mean_ready, j + 1)
                n = c.stop - c.start
                a.activation(rs[:, 0:n], rtmp[:, 0:n], ACT.Sqrt).then_inc(rs_ready, 1)
                if whole == 2:
                    for kt in range(KT):
                        high(kt)

            split_high(UNITS)
            norm(0, whole=2)
            for m in range(KT):
                pb = wait_group(act, f"q{m}")
                split_high()
                a.activation(qT[:, m, :], pb[:, 0:SEQ], ACT.Copy, scale=HD ** -0.5).then_inc(free(f"q{m}"), 1)
            split_high(UNIT["wo"] - KT)
            a.preload_act_table_set("natural_log_exp_and_others")
            for i in range(HEADS + 1):
                if i < HEADS:
                    pb = wait_group(act, f"z{i}")
                    if i >= 2:
                        act.wait_ge(sp_ready, i - 1)
                    t = lnz[:, i % 2, :]
                    link(a.activation(t, pb[:, 0:384], ACT.Abs))
                    link(a.activation(t, t, ACT.Exp, scale=-1.0))
                    a.activation(t, t, ACT.Ln, bias=1.0).then_inc(lnz_ready, 1)
                if i >= 1:
                    h = i - 1
                    act.wait_ge(cum_done, h + 1)
                    if h >= 2:
                        if h % 2:
                            wait_group(act, f"o{(h - 2) // 2}")
                        else:
                            act.wait_ge(o_done, h // 2)
                    a.activation(wexp[:, h % 2, :], bank[plan.at[f"z{h}"][1]][:, 0:384],
                                 ACT.Exp).then_inc(free(f"z{h}"), 1)
            norm(1, whole=1, units=True)
            split_mlp(0)
            wait_out(act, "par")
            lam = par[:, 12 * KT:13 * KT]
            link(a.activation(lamc[:, 0, :], lam, ACT.Abs))
            link(a.activation(lamc[:, 1, :], lamc[:, 0, :], ACT.Exp, scale=-1.0))
            a.activation(lamc[:, 2, :], lamc[:, 1, :], ACT.Ln, bias=1.0).then_inc(lam_ready, 1)
            norm(2, whole=2, after=UNITS)
            act.wait_ge(xc_ready, 1)
            for m in range(KT):
                pb = wait_group(act, f"rg{m}")
                split_high()
                a.activation(xraw[:, m, CONV - 1:], pb[:, 0:SEQ], ACT.Copy).then_inc(free(f"rg{m}"), 1)
            for m in range(KT):
                pb = wait_group(act, f"rg{KT + m}")
                split_high()
                a.activation(gate[:, m, :], pb[:, 0:SEQ], ACT.Gelu_apprx_tanh).then_inc(free(f"rg{KT + m}"), 1)
            for m in range(KT):
                pb = wait_group(act, f"ri{m}")
                a.activation(rS[:, m, :], pb[:, 0:SEQ], ACT.Sigmoid,
                             bias=par[:, 10 * KT + m:10 * KT + m + 1]).then_inc(ri_ready, 1)
                a.activation(iS[:, m, :], pb[:, SEQ:2 * SEQ], ACT.Sigmoid,
                             bias=par[:, 11 * KT + m:11 * KT + m + 1]).then_inc(free(f"ri{m}"), 1)
            act.wait_ge(ri_ready, KT)
            act.wait_ge(lam_ready, 2)
            for m in range(KT):
                a.activation(aS[:, m, :], rS[:, m, :], ACT.Exp, scale=lamc[:, 4, m:m + 1]).then_inc(at_ready, 1)
                a.activation(tS[:, m, :], rS[:, m, :], ACT.Tanh, scale=lamc[:, 3, m:m + 1]).then_inc(at_ready, 1)
            for m in range(2):
                act.wait_ge(m_ready, m + 1)
                h4 = slice(4 * m, 4 * m + 4)
                a.activation(mS[:, h4], mS[:, h4], ACT.Sqrt).then_inc(mroot_ready, 1)
            for m in range(2):
                act.wait_ge(y_ready, m + 1)
                h4 = slice(4 * m, 4 * m + 4)
                a.activation(m_hl[0][:, h4, :], gate[:, h4, :], ACT.Copy).then_inc(gate_high, 1)
            norm(3, whole=1, units=True)
            split_mlp(1)
            norm(4, after=UNITS)
            norm(5, whole=2)
            act.wait_ge(zf_ready, 1)
            for m in range(ZT):
                pb = wait_group(act, f"zr{m}")
                split_high()
                a.activation(zr[:, m, 1:], pb[:, 0:TOK], ACT.Copy).then_inc(free(f"zr{m}"), 1)
            act.wait_ge(zf_ready, 2)
            a.activation(tlw[0:64], zf[0:64, 12, :], ACT.Tanh).then_inc(lw_ready, 1)
            a.activation(slg, zf[:, 13, CH:WT], ACT.Sigmoid).then_inc(lw_ready, 1)
            for m in range(RT):
                pb = wait_group(act, f"wp{m}")
                a.activation(ld[:, m, :], pb[:, 0:WT], ACT.Sigmoid,
                             bias=par[:, 268 + m:269 + m]).then_inc(free(f"wp{m}"), 1)
            for m in range(RT):
                pb = wait_group(act, f"ap{m}")
                a.activation(aa[:, m, :], pb[:, 0:WT], ACT.Sigmoid,
                             bias=par[:, 272 + m:273 + m]).then_inc(free(f"ap{m}"), 1)
            for m in range(RT):
                pb = wait_group(act, f"gp{m}")
                a.activation(gg[:, m, :], pb[:, 0:SEQ], ACT.Copy).then_inc(free(f"gp{m}"), 1)
            act.wait_ge(kkn_ready, 1)
            a.activation(Kh, Bh, ACT.Sqrt).then_inc(ksq_ready, 1)
            act.wait_ge(lp_ready, 1)
            link(a.activation(Pd, LP, ACT.Exp))
            act.wait_ge(lp_ready, 2)
            link(a.activation(Pi, LP, ACT.Exp, scale=-1.0))
            a.activation(ld, ld, ACT.Exp).then_inc(p_ready, 1)
            for m in range(RT):
                pb = wait_group(act, f"val{m}")
                split_high()
                a.activation(val[:, m, :], pb[:, 0:TOK], ACT.Copy).then_inc(free(f"val{m}"), 1)
            for m in range(RT):
                pb = wait_group(act, f"cg{m}")
                a.activation(cg[:, m, :], pb[:, 0:TOK], ACT.Sigmoid).then_inc(free(f"cg{m}"), 1)
            act.wait_ge(zf_ready, 3)
            for tt in range(3):
                n = CH if tt == 0 else P
                for s_ in range(3):
                    pb = wait_group(act, f"nat{s_}_{tt}")
                    a.activation(nat[s_][0:n, tt, :], pb[0:n, :], ACT.Copy,
                                 scale=-1.0 if s_ == 2 else 1.0).then_inc(free(f"nat{s_}_{tt}"), 1)
            for lv in range(1, LEVELS):
                for tt in range(3):
                    n = CH if tt == 0 else P
                    pb = wait_group(act, f"Y{lv}_{tt}")
                    a.activation(Y[0:n, tt].rearrange("p h s -> p (h s)"), pb[0:n, :],
                                 ACT.Copy).then_inc(free(f"Y{lv}_{tt}"), 1)
            for tt in range(3):
                n = CH if tt == 0 else P
                pb = wait_group(act, f"GV_{tt}")
                a.activation(G1[0:n, tt].rearrange("p h s -> p (h s)"), pb[0:n, :], ACT.Copy).then_inc(free(f"GV_{tt}"), 1)
            for c in range(NCH):
                p0 = CH * ((c - 1) % 2) if c else 0
                if c:
                    pb = wait_group(act, f"OA_{c}")
                    a.activation(owk[:, :, (c - 1) * CH:c * CH],
                                      pb[:, 0:RT * CH].rearrange("p (q t) -> p q t", t=CH), ACT.Copy).then_inc(free(f"OA_{c}"), 1)
                pb = wait_group(act, f"U_{c}")
                a.activation(Uc[p0:p0 + CH].rearrange("p h v -> p (h v)"), pb[p0:p0 + CH, :], ACT.Copy).then_inc(free(f"U_{c}"), 1)
            act.wait_ge(owk_ready, 1)
            split_high(UNITS)
            act.wait_ge(osq_ready, 2)
            a.activation(orr, orr, ACT.Sqrt).then_inc(rs_ready, 1)

            def gates(first, count):
                for m in range(first, first + count):
                    pb = wait_group(act, f"gl{m}")
                    split_high()
                    a.activation(GAB[:, m, :], pb[:, 0:SEQ], ACT.Sigmoid).then_inc(free(f"gl{m}"), 1)

            gates(0, KT)
            act.wait_ge(yb_in, 1)
            a.activation(y_hl[0][:, 0:RT, :], owk, ACT.Copy).then_inc(y_high, 1)
            act.wait_ge(csq_ready, 2)
            a.activation(rs[:, 0:SEQ], rtmp[:, 0:SEQ], ACT.Sqrt).then_inc(rs_ready, 1)
            gates(KT, KT // 2)
            act.wait_ge(cin_ready, 1)
            a.activation(ct, cy, ACT.Sigmoid).then_inc(cin_sig, 1)
            act.wait_ge(cin_sig, 2)
            a.activation(y_hl[0][:, RT:2 * RT, :], cy, ACT.Copy).then_inc(y_high, 1)
            gates(KT + KT // 2, KT // 2)
            split_high(UNITS)
            for m in range(KT):
                if m % 2:
                    split_high()
                act.wait_ge(mix_ready, m + 1)
                a.activation(h_hl[0][:, m, real], mix[:, m, :], ACT.Copy).then_inc(mix_high, 1)
            norm(6, whole=2, units=True)

            def finish(tt):
                act.wait_ge(y_ready2, 2 * tt + 1)
                a.activation(junk, yacc, ACT.Square, accum_out=fsq[:, 0:1]).then_inc(fsum_ready, 1)
                act.wait_ge(y_ready2, 2 * tt + 2)
                a.activation(fsq[:, 2:3], fsq[:, 1:2], ACT.Sqrt).then_inc(fsum_ready, 1)

            for m in range(2 * PH):
                pb = wait_group(act, f"pq{m}")
                if m < 2 * PH - UNITS:
                    split_high()
                a.activation(pq[:, m, :], pb[:, 0:SEQ], ACT.Copy).then_inc(free(f"pq{m}"), 1)
            for tt in range(2):
                for dst, nm in ((fnat, "xn"), (hnat, "hn")):
                    for m in range(2):
                        pb = wait_group(act, f"{nm}{tt}_{m}")
                        a.activation(dst[:, tt, 512 * m:512 * (m + 1)], pb[:, :], ACT.Copy).then_inc(free(f"{nm}{tt}_{m}"), 1)
            wait_group(act, "sc1_3")
            for tt in range(2):
                for m in range(4):
                    act.wait_ge(gsel_ready, 4 * tt + m + 1)
                    g3 = gsel[:, tt, 2 * TOPK * m:2 * TOPK * (m + 1)]
                    a.activation(g3, g3, ACT.Exp).then_inc(gsel_exp, 1)
                if tt:
                    act.wait_ge(eidx_ready, 8)
                    act.dma_start(gfin, g_final.partition_broadcast(P)).then_inc(gfin_loaded, 16)
                    finish(0)
                act.wait_ge(dots_ready, tt + 1)
                a.activation(coef[:, tt, :], dots[:, tt, :], ACT.Gelu).then_inc(gelu_ready, 1)
                with act.Fori(0, SEL // GR, 1) as i:
                    act.wait_ge(coef_copied, i + (SEL // GR * tt + 1))
                    for k, j in enumerate(PE_ROWS):
                        a.activation(diag[:, k, :], ident[:], ACT.Copy,
                                     scale=coef16[:, j:j + 1]).then_inc(diag_ready, 1)
            finish(1)

        @block.vector
        def _(dve):
            chain = [0]
            v = nc.vector

            def link(ins):
                chain[0] += 1
                ins.then_inc(dve_chain, 1)
                dve.wait_ge(dve_chain, chain[0])

            def mark(ins):
                chain[0] += 1
                ins.then_inc(dve_chain, 1)

            def settle():
                dve.wait_ge(dve_chain, chain[0])

            def pc(i, m):
                return par[:, i * KT + m:i * KT + m + 1]

            def pr(i, m):
                return par[:, 256 + RT * i + m:257 + RT * i + m]

            def norm(j, gain=None, dst=hT):
                c = norm_cols(j)
                n = c.stop - c.start
                pb = wait_group(dve, f"ms{j}")
                link(v.tensor_scalar(rtmp[:, 0:n], pb[:, 0:n], EPS, None, ALU.add))
                link(v.reciprocal(rtmp[:, 0:n], rtmp[:, 0:n]))
                dve.sem_inc(free(f"ms{j}"), 1)
                dve.sem_inc(mean_ready, 1)
                dve.wait_ge(rs_ready, RS_AT[j])
                if gain is None:
                    return
                for kt in range(KT):
                    ins = v.scalar_tensor_tensor(dst[:, kt, c], xT[:, kt, c], pc(gain, kt), rs[:, 0:n],
                                                 ALU.mult, ALU.mult)
                    ins.then_inc(h_whole if dst is hT else x_ready, 1)
                    if dst is hT and kt >= 2:
                        low(j, hT[:, :, c], [kt - 2])
                if dst is hT:
                    low(j, hT[:, :, c], [KT - 2, KT - 1])

            def low(j, whole, kts=range(KT)):
                for kt in kts:
                    dve.wait_ge(h_high, KT * H_AT[j] + kt + 1)
                    v.tensor_tensor(h_hl[1][:, kt, norm_cols(j)], whole[:, kt, :],
                                    h_hl[0][:, kt, norm_cols(j)].bitcast(F32), ALU.subtract).then_inc(h_ready, 1)

            def residual(names, mlp_norm=None):
                for kt, name in enumerate(names):
                    pb = wait_group(dve, name)
                    link(v.tensor_tensor(xT[:, kt, real], xT[:, kt, real], pb[:, 0:SEQ], ALU.add))
                    dve.sem_inc(free(name), 1)
                    dve.sem_inc(x_ready, 1)
                    if mlp_norm is not None:
                        v.tensor_scalar(xg[:, kt, :], xT[:, kt, real], pc((mlp_norm + 3) // 2, kt), None,
                                        ALU.mult).then_inc(h_whole, 1)
                if mlp_norm is not None:
                    low(mlp_norm, xg)

            for kt in range(KT):
                pb = wait_group(dve, f"xT{kt}")
                link(v.tensor_copy(xT[:, kt, :], pb[:, 0:TOK]))
                dve.sem_inc(free(f"xT{kt}"), 1)
                dve.sem_inc(x_ready, 1)
            pb = wait_group(dve, "par")
            mark(v.tensor_copy(par[:, 0:15 * KT], pb[:, 0:15 * KT]))
            mark(v.tensor_copy(par[:, 128:128 + CK * RT], pb[:, 128:128 + CK * RT]))
            mark(v.tensor_copy(par[:, 256:256 + 10 * RT + ZT], pb[:, 256:256 + 10 * RT + ZT]))
            settle()
            dve.sem_inc(free("par"), 1)
            norm(0, 0)
            for m in range(KT):
                pb = wait_group(dve, f"k{m}")
                v.tensor_copy(kT[:, m, :], pb[:, 0:SEQ]).then_inc(free(f"k{m}"), 1)
            for j in range(4):
                for tt in range(2):
                    pb = wait_group(dve, f"v{j}_{tt}")
                    v.tensor_copy(V[:, tt, 256 * j:256 * (j + 1)], pb[:, 0:256]).then_inc(free(f"v{j}_{tt}"), 1)
            dve.wait_ge(consts_built, 2)
            for i in range(HEADS + 3):
                if i < HEADS:
                    dve.wait_ge(lnz_ready, i + 1)
                    if i >= 2:
                        dve.wait_ge(cum_done, i - 1)
                    link(v.scalar_tensor_tensor(sp[:, i % 2, :], bank[plan.at[f"z{i}"][1]][:, 0:384], 0.0,
                                                lnz[:, i % 2, :], ALU.max, ALU.add))
                    v.tensor_tensor(sp[:, i % 2, :], sp[:, i % 2, :], attn_mask[:], ALU.mult).then_inc(sp_ready, 1)
                if 1 <= i <= HEADS:
                    h = i - 1
                    wait_out(dve, f"z{h}")
                    v.scalar_tensor_tensor(wexp[:, h % 2, :], wexp[:, h % 2, :], 2.0, attn_mask[:],
                                           ALU.min, ALU.mult).then_inc(w_ready, 1)
                if i >= 3 and i % 2 == 1:
                    q = (i - 3) // 2
                    pb = wait_group(dve, f"o{q}")
                    high, low_ = (h[:, q, :] for h in m_hl)
                    link(v.tensor_copy(high, pb[:, 0:SEQ]))
                    v.tensor_tensor(low_, pb[:, 0:SEQ], high.bitcast(F32), ALU.subtract).then_inc(free(f"o{q}"), 1)
            residual([f"wo{m}" for m in range(KT)], mlp_norm=1)

            def mlp(layer):
                n0, banks, used = plan.at[f"up{layer}"]
                with dve.Fori(0, 4, 1) as i:
                    for j in range(BANKS):
                        dve.wait_ge(group_done, i * BANKS + (n0 + j + 1))
                        def step(k):
                            dve.wait_ge(u_step, i * (3 * BANKS) + (3 * (FF // P * layer + j) + k))

                        t, u_ = utmp[:, j % 2, :], utmp[:, 2 + j % 2, :]
                        high, low = (u_hl[part][:, bass.ds(i * BANKS + j, 1), :].rearrange("p a b -> p (a b)")
                                     for part in range(2))
                        v.scalar_tensor_tensor(t, bank[banks[j]][:, 0:SEQ], 0.0, rs[:, 0:SEQ], ALU.max,
                                               ALU.mult).then_inc(bank_free[banks[j]], 1)
                        dve.wait_ge(bank_free[banks[j]], i + (used[j] + 1))
                        v.tensor_tensor(u_, t, t, ALU.mult).then_inc(u_step, 1)
                        step(1)
                        v.tensor_copy(high, u_).then_inc(u_step, 1)
                        step(2)
                        v.tensor_tensor(low, u_, high.bitcast(F32), ALU.subtract).then_inc(u_step, 1)
                n0, banks, used = plan.at[f"down{layer}"]
                with dve.Fori(0, 2, 1) as i:
                    for j in range(4):
                        dve.wait_ge(group_done, i * 16 + (n0 + 8 * (j // 2) + 6 + j % 2 + 1))
                        xs = xT[:, i * 4 + j, real]
                        v.tensor_tensor(xs, xs, bank[banks[j]][:, 0:SEQ], ALU.add).then_inc(x_ready, 1)
                        dve.wait_ge(x_ready, i * 4 + (KT * (2 + 2 * layer) + j + 1))
                        dve.sem_inc(bank_free[banks[j]], 1)

            norm(1)
            mlp(0)
            dve.wait_ge(lam_ready, 1)
            link(v.tensor_scalar(lamc[:, 3, :], par[:, 12 * KT:13 * KT], -1.0, 0.0, ALU.mult, ALU.max))
            link(v.tensor_tensor(lamc[:, 3, :], lamc[:, 3, :], lamc[:, 2, :], ALU.add))
            link(v.tensor_scalar(lamc[:, 3, :], lamc[:, 3, :], 8.0, None, ALU.mult))
            link(v.tensor_scalar(lamc[:, 4, :], lamc[:, 3, :], -1.0, None, ALU.mult))
            dve.sem_inc(lam_ready, 1)
            v.memset(xraw[:, :, 0:CONV - 1], 0.0).then_inc(xc_ready, 1)
            norm(2, 1)
            for m in range(KT):
                wait_out(dve, f"rg{m}")
                link(v.tensor_scalar(xc[:, m, :], xraw[:, m, 0:SEQ], pc(5, m), pc(9, m), ALU.mult, ALU.add))
                for t in range(1, CONV):
                    link(v.scalar_tensor_tensor(xc[:, m, :], xraw[:, m, t:t + SEQ], pc(5 + t, m),
                                                xc[:, m, :], ALU.mult, ALU.add))
                dve.sem_inc(xc_ready, 1)
            for m in range(KT):
                wait_out(dve, f"ri{m}")
                mark(v.tensor_tensor(iS[:, m, :], iS[:, m, :], xc[:, m, :], ALU.mult))
            halves = [slice(0, KT // 2), slice(KT // 2, KT)]
            for m, h4 in enumerate(halves):
                dve.wait_ge(at_ready, KT * (m + 1))
                link(v.tensor_scalar(mS[:, h4], tS[:, h4], 1.0, None, ALU.add))
                link(v.reciprocal(mS[:, h4], mS[:, h4]))
                link(v.scalar_tensor_tensor(mS[:, h4].rearrange("p a b -> p (a b)"),
                                            tS[:, h4].rearrange("p a b -> p (a b)"), 2.0,
                                            mS[:, h4].rearrange("p a b -> p (a b)"), ALU.mult, ALU.mult))
                dve.sem_inc(m_ready, 1)
            for m, h4 in enumerate(halves):
                dve.wait_ge(mroot_ready, m + 1)
                link(v.tensor_tensor(iS[:, h4], iS[:, h4], mS[:, h4], ALU.mult))
                for k in range(h4.start, h4.stop):
                    mark(v.tensor_tensor_scan(rS[:, k, :], aS[:, k, :], iS[:, k, :], 0.0, ALU.mult, ALU.add))
                settle()
                wait_out(dve, *[f"rg{KT + k}" for k in range(h4.start, h4.stop)])
                v.tensor_tensor(gate[:, h4], gate[:, h4], rS[:, h4], ALU.mult).then_inc(y_ready, 1)
            for m in range(2):
                h4 = slice(4 * m, 4 * m + 4)
                dve.wait_ge(gate_high, m + 1)
                v.tensor_tensor(m_hl[1][:, h4], gate[:, h4], m_hl[0][:, h4].bitcast(F32),
                                ALU.subtract).then_inc(y_split, 1)
            residual([f"rgo{m}" for m in range(KT)], mlp_norm=3)
            norm(3)
            mlp(1)
            norm(4, 4, xT)
            v.memset(zf[:, :, 0:PADC], 0.0).then_inc(dve_chain, 1)
            chain[0] += 1
            mark(v.memset(U[:, :, 0:CK - 1], 0.0))
            mark(v.memset(zr[:, :, 0:1], 0.0))
            settle()
            dve.sem_inc(zf_ready, 1)
            norm(5, 13)
            for m in range(ZT):
                wait_out(dve, f"zr{m}")
                z = zf[:, m, PADC:]
                link(v.tensor_tensor(z, zr[:, m, 0:TOK], zr[:, m, 1:], ALU.subtract))
                mark(v.scalar_tensor_tensor(z, z, par[:, 296 + m:297 + m], zr[:, m, 1:], ALU.mult, ALU.add))
            settle()
            dve.sem_inc(zf_ready, 1)
            for m in range(RT):
                mark(v.tensor_scalar(kk[:, m, :], kZ[:, m, :], pr(5, m), None, ALU.mult))
            settle()
            v.tensor_tensor(Kh, kk, kk, ALU.mult).then_inc(kks_ready, 1)
            link(v.tensor_scalar(omka[:], par[:, 280:284], -1.0, 1.0, ALU.mult, ALU.add))
            for m in range(RT):
                pb = wait_group(dve, f"kks{m}")
                v.tensor_scalar(Bh[:, m, :], pb[:, 0:WT], 1e-24, None, ALU.max).then_inc(free(f"kks{m}"), 1)
            wait_out(dve, *[f"kks{m}" for m in range(RT)])
            link(v.reciprocal(Bh, Bh))
            dve.sem_inc(kkn_ready, 1)
            wait_out(dve, *[f"wp{m}" for m in range(RT)])
            link(v.tensor_scalar(ld, ld, DECAY, None, ALU.mult))
            dve.wait_ge(consts_built, 3)
            for m in range(RT):
                mark(v.tensor_tensor_scan(LP[:, m, :], reset[:], ld[:, m, :], 0.0, ALU.mult, ALU.add))
            settle()
            dve.sem_inc(lp_ready, 1)
            link(v.tensor_tensor(ld, LP, ld, ALU.subtract))
            dve.sem_inc(lp_ready, 1)
            dve.wait_ge(ksq_ready, 1)
            link(v.tensor_tensor(kk, kk, Kh, ALU.mult))
            wait_out(dve, *[f"ap{m}" for m in range(RT)])
            for m in range(RT):
                mark(v.tensor_scalar(Bh[:, m, :], aa[:, m, :], pr(6, m), omka[:, m:m + 1], ALU.mult, ALU.add))
            settle()
            link(v.tensor_tensor(kZ, kZ, Bh, ALU.mult))
            link(v.tensor_tensor(Kh, rZ, kZ, ALU.mult))
            for m in range(RT):
                mark(v.tensor_scalar(Kh[:, m, :], Kh[:, m, :], pr(7, m), None, ALU.mult))
            settle()
            dve.sem_inc(rk_ready, 1)
            for m in range(RT):
                pb = wait_group(dve, f"bon{m}")
                v.tensor_tensor(bonus[:, m, :], vZ[:, m, CH:WT], pb[:, 0:SEQ], ALU.mult).then_inc(free(f"bon{m}"), 1)
            wait_out(dve, *[f"bon{m}" for m in range(RT)])
            dve.wait_ge(p_ready, 1)
            mark(v.tensor_tensor(aa, aa, kk, ALU.mult))
            mark(v.tensor_tensor(rZ, rZ, Pd, ALU.mult))
            mark(v.tensor_tensor(kZ, kZ, Pi, ALU.mult))
            settle()
            mark(v.tensor_tensor(aa, aa, Pi, ALU.mult))
            mark(v.tensor_tensor(kk, kk, ld, ALU.mult))
            ends = Pd.rearrange("p m (c j) -> p (m c) j", j=CH)[:, :, CH - 1:CH]
            mark(v.tensor_copy(pend[:].rearrange("p m c -> p (m c)").unsqueeze(2), ends))
            settle()

            def chunks(t):
                return t.rearrange("p m (c j) -> p (m c) j", j=CH)

            pend_b = pend[:].rearrange("p m c -> p (m c)").unsqueeze(2).broadcast_to([P, RT * NCH, CH])
            mark(v.tensor_tensor(chunks(Kh), chunks(kZ), pend_b, ALU.mult))
            mark(v.tensor_tensor(chunks(Bh), chunks(aa), pend_b, ALU.mult))
            settle()
            dve.sem_inc(kb_ready, 1)
            wait_out(dve, *[f"val{m}" for m in range(RT)], *[f"cg{m}" for m in range(RT)])
            link(v.tensor_tensor(U[:, :, CK - 1:], val, cg, ALU.mult))
            dve.sem_inc(zf_ready, 1)

            tap = [0]

            def taps(count):
                for t in range(tap[0], min(tap[0] + count, CK)):
                    settle()
                    for m in range(RT):
                        u_ = U[:, m, META + t:META + t + SEQ]
                        w_ = par[:, 128 + RT * t + m:129 + RT * t + m]
                        if t == 0:
                            mark(v.tensor_scalar(cy[:, m, :], u_, w_, pr(0, m), ALU.mult, ALU.add))
                        else:
                            mark(v.scalar_tensor_tensor(cy[:, m, :], u_, w_, cy[:, m, :], ALU.mult, ALU.add))
                    if t == CK - 1:
                        settle()
                        dve.sem_inc(cy_ready, 1)
                tap[0] += count

            wait_out(dve, *[f"nat{s_}_{tt}" for tt in range(3) for s_ in range(3)])
            def block_of(dst, src, which, tt):
                n = CH if tt == 0 else P
                return v.tensor_tensor(dst[0:n, tt], src[0:n, tt],
                                       lvl[0:n, which, :].unsqueeze(1).broadcast_to([n, RH, CH]), ALU.mult)

            def start_inverse(tt):
                n = CH if tt == 0 else P
                eye_b = eye[0:n].unsqueeze(1).broadcast_to([n, RH, CH])
                for dst, src, which in ((X, Nm, 0), (XT, NT, LEVELS)):
                    link(block_of(dst, src, which, tt))
                    link(v.tensor_tensor(dst[0:n, tt], eye_b, dst[0:n, tt], ALU.subtract))
                link(block_of(MT, NT, LEVELS + 1, tt))
                dve.sem_inc(mt_ready, 1)

            for tt in range(3):
                n = CH if tt == 0 else P
                for s_ in range(5 if tt else 3):
                    dst, mask = ((NT[0:n, tt], strict), (Nm[0:n, tt], lower), (G1[0:n, tt], strict),
                                 (G2[0:n, max(tt - 1, 0)], incl), (G3[0:n, max(tt - 1, 0)], nincl))[s_]
                    dst = dst.rearrange("p (q two) t -> p two q t", two=2)
                    for par_ in range(2):
                        pb = wait_group(dve, f"mat{s_}_{par_}_{tt}")
                        v.tensor_tensor(dst[:, par_], pb[0:n, 0:256].rearrange("p (q t) -> p q t", t=CH),
                                        mask[0:n].unsqueeze(1).broadcast_to([n, 4, CH]),
                                        ALU.mult).then_inc(free(f"mat{s_}_{par_}_{tt}"), 1)
                wait_out(dve, *[f"mat{s_}_{par_}_{tt}" for s_ in range(2) for par_ in range(2)])
                start_inverse(tt)

            for lv in range(1, LEVELS):
                for tt in range(3):
                    n = CH if tt == 0 else P
                    if lv < LEVELS - 1:
                        pb = wait_group(dve, f"XY{lv}_{tt}")
                        xx = X[0:n, tt].rearrange("p h s -> p (h s)")
                        v.tensor_tensor(xx, xx, pb[0:n, :], ALU.subtract).then_inc(free(f"XY{lv}_{tt}"), 1)
                    pb = wait_group(dve, f"YX{lv}_{tt}")
                    xx = XT[0:n, tt].rearrange("p h s -> p (h s)")
                    v.tensor_tensor(xx, xx, pb[0:n, :], ALU.subtract).then_inc(free(f"YX{lv}_{tt}"), 1)
                    if lv < LEVELS - 1:
                        link(block_of(MT, NT, LEVELS + lv + 1, tt))
                        dve.sem_inc(mt_ready, 1)
                    taps(2)
            dve.wait_ge(group_done, plan.at["GV_2"][0])
            wait_out(dve, *[f"GV_{tt}" for tt in range(3)])
            for c in range(NCH):
                tt = (c + 1) // 2
                p0 = CH * ((c - 1) % 2) if c else 0
                rows_ = slice(p0, p0 + CH)
                if c == 0:
                    link(v.tensor_copy(Yc[rows_], G1[rows_, 0]))
                else:
                    for par_ in range(2):
                        pb = wait_group(dve, f"SA{par_}_{c}")
                        yv = Yc[rows_].rearrange("p (q two) t -> p two q t", two=2)[:, par_]
                        gv = G1[rows_, tt].rearrange("p (q two) t -> p two q t", two=2)[:, par_]
                        link(v.tensor_tensor(yv, gv, pb[rows_, 0:256].rearrange("p (q t) -> p q t", t=CH), ALU.add))
                        dve.sem_inc(free(f"SA{par_}_{c}"), 1)
                dve.sem_inc(yc_ready, 1)
                new, old = ST[:, (c + 1) % 2], ST[:, c % 2]
                if c:
                    link(v.tensor_tensor(new, old, pend[:, :, c:c + 1].broadcast_to([P, RT, CH]), ALU.mult))
                pb = wait_group(dve, f"S_{c}")
                pv = pb[:, 0:RT * CH].rearrange("p (q t) -> p q t", t=CH)
                if c:
                    link(v.tensor_tensor(new, new, pv, ALU.add))
                else:
                    link(v.tensor_copy(new, pv))
                dve.sem_inc(free(f"S_{c}"), 1)
                dve.sem_inc(st_ready, 1)
                taps(1)
                if c:
                    pb = wait_group(dve, f"OB_{c}")
                    wait_out(dve, f"OA_{c}")
                    ov = owk[:, :, (c - 1) * CH:c * CH]
                    link(v.tensor_tensor(ov, ov, pb[:, 0:RT * CH].rearrange("p (q t) -> p q t", t=CH), ALU.add))
                    dve.sem_inc(free(f"OB_{c}"), 1)
            dve.sem_inc(owk_ready, 1)
            for m in range(RT):
                pb = wait_group(dve, f"gm{m}")
                link(v.tensor_tensor(owk[:, m, :], owk[:, m, :], pb[:, 0:SEQ], ALU.subtract))
                dve.sem_inc(free(f"gm{m}"), 1)
            link(v.tensor_tensor(osq, owk, owk, ALU.mult))
            dve.sem_inc(osq_ready, 1)
            for m in range(RT):
                pb = wait_group(dve, f"gv{m}")
                link(v.tensor_scalar(orr[:, m, :], pb[:, 0:SEQ], GN_EPS, None, ALU.add))
                dve.sem_inc(free(f"gv{m}"), 1)
            link(v.reciprocal(orr, orr))
            dve.sem_inc(osq_ready, 1)
            taps(CK)
            pb = wait_group(dve, "lm")
            link(v.tensor_tensor(cy, cy, pb[:, 0:SEQ].unsqueeze(1).broadcast_to([P, RT, SEQ]), ALU.subtract))
            dve.sem_inc(free("lm"), 1)
            link(v.tensor_tensor(ct, cy, cy, ALU.mult))
            dve.sem_inc(csq_ready, 1)
            dve.wait_ge(rs_ready, RS_AT["gn"])
            link(v.tensor_tensor(owk, owk, orr, ALU.mult))
            for m in range(RT):
                mark(v.tensor_scalar(owk[:, m, :], owk[:, m, :], pr(8, m), pr(9, m), ALU.mult, ALU.add))
            settle()
            link(v.tensor_tensor(owk, owk, bonus, ALU.add))
            wait_out(dve, *[f"gp{m}" for m in range(RT)])
            link(v.tensor_tensor(owk, owk, gg, ALU.mult))
            dve.sem_inc(yb_in, 1)

            def split_branch(i):
                part = slice(RT * i, RT * (i + 1))
                dve.wait_ge(y_high, i + 1)
                v.tensor_tensor(y_hl[1][:, part, :], (owk, cy)[i], y_hl[0][:, part, :].bitcast(F32),
                                ALU.subtract).then_inc(y_split, 1)

            split_branch(0)
            pb = wait_group(dve, "lv")
            link(v.tensor_scalar(rtmp[:, 0:SEQ], pb[:, 0:SEQ], LN_EPS, None, ALU.add))
            link(v.reciprocal(rtmp[:, 0:SEQ], rtmp[:, 0:SEQ]))
            dve.sem_inc(free("lv"), 1)
            dve.sem_inc(csq_ready, 1)
            dve.wait_ge(rs_ready, RS_AT["ln"])
            link(v.tensor_tensor(cy, cy, rs[:, 0:SEQ].unsqueeze(1).broadcast_to([P, RT, SEQ]), ALU.mult))
            for m in range(RT):
                mark(v.tensor_scalar(cy[:, m, :], cy[:, m, :], pr(1, m), pr(2, m), ALU.mult, ALU.add))
            settle()
            dve.sem_inc(cin_ready, 1)
            dve.wait_ge(cin_sig, 1)
            link(v.tensor_tensor(cy, cy, ct, ALU.mult))
            dve.sem_inc(cin_sig, 1)
            split_branch(1)
            wait_out(dve, *[f"gl{m}" for m in range(2 * KT)][KT:])
            for m in range(KT):
                pb = wait_group(dve, f"yb{m}")
                v.tensor_tensor(mix[:, m, :], pb[:, 0:SEQ], GAB[:, KT + m, :], ALU.mult).then_inc(free(f"yb{m}"), 1)
            for m in range(KT):
                pb = wait_group(dve, f"ya{m}")
                link(v.tensor_tensor(mt2, pb[:, 0:SEQ], GAB[:, m, :], ALU.mult))
                dve.sem_inc(free(f"ya{m}"), 1)
                v.tensor_tensor(mix[:, m, :], mix[:, m, :], mt2, ALU.add).then_inc(mix_ready, 1)
                dve.wait_ge(mix_ready, m + 1)
            for m in range(KT):
                dve.wait_ge(mix_high, m + 1)
                v.tensor_tensor(h_hl[1][:, m, real], mix[:, m, :], h_hl[0][:, m, real].bitcast(F32),
                                ALU.subtract).then_inc(mix_split, 1)
            residual([f"wo2{m}" for m in range(KT)])
            norm(6, 14)
            for m in range(4):
                pb = wait_group(dve, f"key{m}")
                v.tensor_copy(keyT[:, 4 * m:4 * m + 4, :].rearrange("p a n -> p (a n)"),
                              pb[:, :]).then_inc(free(f"key{m}"), 1)

            def top16(vals, idx, src, rest):
                for r_ in range(src.shape[1]):
                    mark(v.max(vals[:, r_, 0:8], src[:, r_, :]))
                settle()
                for r_ in range(src.shape[1]):
                    mark(v.max_index(idx[:, r_, 0:8], vals[:, r_, 0:8], src[:, r_, :]))
                    mark(v.match_replace(rest[:, r_, :], vals[:, r_, 0:8], src[:, r_, :], NEG))
                settle()
                for r_ in range(src.shape[1]):
                    mark(v.max(vals[:, r_, 8:16], rest[:, r_, :]))
                settle()
                for r_ in range(src.shape[1]):
                    mark(v.max_index(idx[:, r_, 8:16], vals[:, r_, 8:16], rest[:, r_, :]))
                settle()

            def choose(tt, m):
                hs, hc = slice(2 * m, 2 * m + 2), slice(4 * m, 4 * m + 4)
                pb = wait_group(dve, f"sc{tt}_{m}")
                link(v.tensor_copy(sc[:, hc, :].rearrange("p a n -> p (a n)"), pb[:, :]))
                dve.sem_inc(free(f"sc{tt}_{m}"), 1)
                top16(topv[:, hc], topi[:, hc], sc[:, hc], sc2[:, hc])
                mark(v.tensor_copy(topf[:, hc], topi[:, hc]))
                for h in (2 * m, 2 * m + 1):
                    mark(v.tensor_tensor(cand[:, h, :].rearrange("p (i j) -> p i j", j=TOPK),
                                         topv[:, 2 * h, :].unsqueeze(2).broadcast_to([P, TOPK, TOPK]),
                                         topv[:, 2 * h + 1, :].unsqueeze(1).broadcast_to([P, TOPK, TOPK]), ALU.add))
                settle()
                top16(bv[:, hs], bi[:, hs], cand[:, hs], cand2[:, hs])
                g3 = gsel[:, tt, :].rearrange("p (h s) -> p h s", s=TOPK)[:, hs]
                link(v.tensor_tensor(g3, bv[:, hs], bv[:, hs, 0:1].broadcast_to([P, 2, TOPK]), ALU.subtract))
                dve.sem_inc(gsel_ready, 1)
                mark(v.tensor_scalar(bt[:, hs], bi[:, hs], 4, None, ALU.logical_shift_right))
                mark(v.tensor_scalar(bt2[:, hs], bi[:, hs], TOPK - 1, None, ALU.bitwise_and))
                settle()
                mark(v.tensor_copy(rowf[:, hs], bt[:, hs]))
                mark(v.tensor_copy(colf[:, hs], bt2[:, hs]))
                settle()
                n = 2 * TOPK
                for src, half, dst in ((rowf, 0, i1f), (colf, 1, i2f)):
                    o_ = oh[:, n * m:n * (m + 1), :]
                    link(v.tensor_tensor(o_, src[:, hs].rearrange("p h s -> p (h s)").unsqueeze(2).broadcast_to([P, n, TOPK]),
                                         io16[:].unsqueeze(1).broadcast_to([P, n, TOPK]), ALU.is_equal))
                    for h in range(2):
                        oo = o_[:, TOPK * h:TOPK * (h + 1), :]
                        mark(v.tensor_tensor(oo, oo, topf[:, 4 * m + 2 * h + half, :].unsqueeze(1).broadcast_to(
                            [P, TOPK, TOPK]), ALU.mult))
                    settle()
                    link(v.tensor_reduce(dst[:, hs].rearrange("p h s -> p (h s)"), o_, AX.X, ALU.add))
                i1, i2 = (t[:, hs].rearrange("p h s -> p (h s)") for t in (i1f, i2f))
                link(v.scalar_tensor_tensor(i1, i1, float(NK), i2, ALU.mult, ALU.add))
                link(v.tensor_copy(eidx[:, tt, n * m:n * (m + 1)], i1))

            def share(tt):
                g3 = gsel[:, tt, :].rearrange("p (h s) -> p h s", s=TOPK)
                dve.wait_ge(gsel_exp, 4 * (tt + 1))
                link(v.tensor_reduce(psm, g3, AX.X, ALU.add))
                link(v.reciprocal(psm, psm))
                link(v.tensor_tensor(g3, g3, psm.unsqueeze(2).broadcast_to([P, PH, TOPK]), ALU.mult))

            def dot_rounds(tt, r0, count):
                first = 2 * tt * (SEL // GR) + r0
                with dve.Fori(0, count, 1) as i:
                    for j in range(GR):
                        dve.wait_ge(row_loaded[j], i * 16 + 16 * (first + 1))
                        v.tensor_tensor_reduce(out=junk, in0=grow(j), in1=fnat[:, tt, :], scale=1.0, scalar=0.0,
                                               op0=ALU.mult, op1=ALU.add,
                                               accum_out=dot16[:, j:j + 1]).then_inc(rows_free, 1)
                        dve.wait_ge(rows_free, i * GR + (GR * (first + 1) + j + 1))
                    v.tensor_copy(dots[:, tt, bass.ds(i * GR + r0 * GR, GR)], dot16).then_inc(dot_saved, 1)
                    dve.wait_ge(dot_saved, i + (SEL // GR * tt + r0 + 1))

            def sum_rounds(tt, r0, count):
                first = (2 * tt + 1) * (SEL // GR) + r0
                n, round0 = len(PE_ROWS), SEL // GR * tt + r0
                with dve.Fori(0, count, 1) as i:
                    v.tensor_copy(coef16, coef[:, tt, bass.ds(i * GR + r0 * GR, GR)]).then_inc(coef_copied, 1)
                    dve.wait_ge(coef_copied, i + (round0 + 1))
                    for j in range(GR):
                        if j in PE_ROWS:
                            continue
                        dve.wait_ge(row_loaded[j], i * 16 + 16 * (first + 1))
                        ins = v.scalar_tensor_tensor(yacc, grow(j), coef16[:, j:j + 1], yacc, ALU.mult, ALU.add)
                        if j - 1 in PE_ROWS:
                            k = PE_ROWS.index(j - 1)
                            ins.then_inc(y_step, 1)
                            dve.wait_ge(y_step, i * n + (n * round0 + k + 1))
                            dve.wait_ge(pe_used, i * n + (n * round0 + k + 1))
                            dve.sem_inc(rows_free, 2)
                        else:
                            ins.then_inc(rows_free, 1)
                            dve.wait_ge(rows_free, i * GR + (GR * (first + 1) + j + 1))

            def pick(tt, m):
                choose(tt, m)
                dve.sem_inc(eidx_ready, 1)

            dve.wait_ge(io_ready, 1)
            pick(0, 0)
            dve.sem_inc(rows_free, GR)
            pick(0, 1)
            for tt in range(2):
                wait_out(dve, *[f"{nm}{tt}_{m}" for nm in ("xn", "hn") for m in range(2)])
                if tt == 0:
                    for m in range(4):
                        dot_rounds(0, 2 * m, 2)
                        if m < 2:
                            pick(0, m + 2)
                else:
                    dot_rounds(1, 0, SEL // GR)
                dve.sem_inc(dots_ready, 1)
                share(tt)
                dve.wait_ge(gelu_ready, tt + 1)
                link(v.tensor_tensor(coef[:, tt, :], coef[:, tt, :], gsel[:, tt, :], ALU.mult))
                if tt:
                    dve.wait_ge(out_written, 16 * tt)
                link(v.memset(yacc, 0.0))
                if tt == 0:
                    for m in range(4):
                        sum_rounds(0, 2 * m, 2)
                        pick(1, m)
                else:
                    sum_rounds(1, 0, SEL // GR)
                for half in range(2):
                    y_ = yacc[:, 512 * half:512 * (half + 1)]
                    mark(v.tensor_tensor(y_, y_, y_banks[tt][half][:, :], ALU.add))
                settle()
                dve.sem_inc(y_ready2, 1)
                dve.wait_ge(fsum_ready, 2 * tt + 1)
                link(v.tensor_scalar(fsq[:, 1:2], fsq[:, 0:1], 1.0 / D, EPS, ALU.mult, ALU.add))
                link(v.reciprocal(fsq[:, 1:2], fsq[:, 1:2]))
                dve.sem_inc(y_ready2, 1)
                dve.wait_ge(fsum_ready, 2 * tt + 2)
                dve.wait_ge(gfin_loaded, 16)
                link(v.scalar_tensor_tensor(yacc, yacc, fsq[:, 2:3], gfin, ALU.mult, ALU.mult))
                dve.sem_inc(fin_ready, 1)

        @block.tensor
        def _(pe):
            mm = nc.tensor.matmul

            def open_bank(name):
                _, b, used = plan.at[name]
                if used:
                    pe.wait_ge(bank_free[b], used)
                return bank[b]

            def transposed(dst, src, n):
                return nc.tensor.transpose(dst, src, ident[0:n, 0:n])

            pe.wait_ge(consts_built, 1)
            pe.wait_ge(x_loaded, 32)
            for kt in range(KT):
                pb = open_bank(f"xT{kt}")
                cols = slice(kt * P, (kt + 1) * P)
                transposed(pb[:, 0:META], metanat[0:META, cols], META)
                for tt in range(2):
                    last = transposed(pb[:, META + tt * P:META + (tt + 1) * P], xnat[:, tt, cols], P)
                last.then_inc(group_done, 1)
            pe.wait_ge(rows_loaded, 16 * N_ROW_DMAS)
            pb = open_bank("par")
            transposed(pb[:, 0:15 * KT], rows[0:15 * KT, 0, :], 15 * KT)
            transposed(pb[:, 128:128 + CK * RT], rows[0:CK * RT, 1, :], CK * RT)
            transposed(pb[:, 256:256 + 10 * RT + ZT], rows[0:10 * RT + ZT, 2, :],
                       10 * RT + ZT).then_inc(group_done, 1)

            def norm(j):
                c = norm_cols(j)
                pb = open_bank(f"ms{j}")
                for kt in range(KT):
                    pe.wait_ge(sq_ready, KT * j + kt + 1)
                    last = mm(pb[:, 0:c.stop - c.start], mean_d[:], sq[:, kt, c], start=kt == 0, stop=kt == KT - 1)
                last.then_inc(group_done, 1)

            def slot(s, cols=256):
                pe.wait_ge(w_loaded[s % RING], 16 * (s // RING + 1))
                return wring[:, s % RING, :].rearrange("p (k n) -> p k n", n=cols)

            def split_unit(n):
                pe.wait_ge(w_split, n + 1)
                return [unit(n, part) for part in range(2)]

            def products(dst, left, right, first, last_):
                mm(dst, left[0], right[0], start=first, stop=False)
                mm(dst, left[0], right[1], start=False, stop=False)
                return mm(dst, left[1], right[0], start=False, stop=last_)

            def project(names, phase, moving, ready=None, first=0):
                for g_, name in enumerate(names):
                    per = 2 if UNITS_OF[UNIT[phase]][2] == "wide" else 1
                    if g_ % per == 0:
                        w = split_unit(UNIT[phase] + first + g_ // per)
                    pb = open_bank(name)
                    kts = w[0].shape[1]
                    for kt in range(kts):
                        if g_ == 0 and ready is not None:
                            pe.wait_ge(*ready(kt))
                        r = moving(kt)
                        last = products(pb[:, 0:r[0].shape[-1]],
                                        [t[:, kt, (g_ % per) * P:(g_ % per + 1) * P] for t in w], r,
                                        kt == 0, kt == kts - 1)
                    last.then_inc(group_done, 1)

            def h_real(kt):
                return [h[:, kt, real] for h in h_hl]

            def h_all(kt):
                return [h[:, kt, :] for h in h_hl]

            def m_all(kt):
                return [m[:, kt, :] for m in m_hl]

            def h_wait(j):
                return lambda kt: (h_ready, KT * H_AT[j] + kt + 1)

            norm(0)
            project([f"q{m}" for m in range(KT)], "qkv", h_real, ready=h_wait(0))
            project([f"k{m}" for m in range(KT)], "qkv", h_real, first=KT)
            for j in range(4):
                banks = [open_bank(f"v{j}_{tt}") for tt in range(2)]
                for half in range(2):
                    w = split_unit(UNIT["qkv"] + 2 * KT + 2 * j + half)
                    for tt in range(2):
                        for k in range(4):
                            kt = 4 * half + k
                            last = products(banks[tt][:, 0:256],
                                            [h[:, kt, META + tt * P:META + (tt + 1) * P] for h in h_hl],
                                            [t[:, k, :] for t in w], kt == 0, kt == KT - 1)
                        if half:
                            last.then_inc(group_done, 1)
            wait_out(pe, *[f"{n}{m}" for n in "qk" for m in range(KT)])
            wait_out(pe, *[f"v{j}_{tt}" for j in range(4) for tt in range(2)])
            for i in range(HEADS + 2):
                if i < HEADS:
                    pb = open_bank(f"z{i}")
                    ch = slice(HD * (i % 2), HD * (i % 2 + 1))
                    mm(pb[:, 0:256], kT[ch, i // 2, 0:P], qT[ch, i // 2, :], start=True, stop=True)
                    mm(pb[:, 256:384], kT[ch, i // 2, P:2 * P], qT[ch, i // 2, P:2 * P], start=False, stop=True,
                       skip_group_check=True).then_inc(group_done, 1)
                if 1 <= i <= HEADS:
                    pe.wait_ge(sp_ready, i)
                    pb = bank[plan.at[f"z{i - 1}"][1]]
                    s_ = sp[:, (i - 1) % 2, :]
                    mm(pb[:, 0:256], neg_tri[:], s_[:, 0:256], start=False, stop=True, skip_group_check=True)
                    mm(pb[:, P:256], neg_one[:], s_[:, 256:384], start=False, stop=True, skip_group_check=True)
                    mm(pb[:, 256:384], neg_tri[:], s_[:, 256:384], start=False, stop=True,
                       skip_group_check=True).then_inc(cum_done, 1)
                if i >= 2:
                    h = i - 2
                    if h % 2 == 0:
                        pb = open_bank(f"o{h // 2}")
                    else:
                        pb = bank[plan.at[f"o{h // 2}"][1]]
                    pe.wait_ge(w_ready, h + 1)
                    o_ = pb[HD * (h % 2):HD * (h % 2 + 1), :]
                    mm(o_[:, 0:256], V[:, 0, h * HD:(h + 1) * HD], wexp[:, h % 2, 0:256], start=True, stop=False)
                    last = mm(o_[:, P:256], V[:, 1, h * HD:(h + 1) * HD], wexp[:, h % 2, 256:384],
                              start=False, stop=True)
                    last.then_inc(group_done if h % 2 else o_done, 1)
            wait_out(pe, *[f"o{q}" for q in range(KT)])
            project([f"wo{m}" for m in range(KT)], "wo", m_all)

            def mlp(layer):
                norm(1 + 2 * layer)
                pe.wait_ge(h_ready, KT * (H_AT[1 + 2 * layer] + 1))
                split0 = UNIT[f"up{layer}"]

                def mlp_products(dst, n, moving, kt, first, last_):
                    return products(dst, [unit(split0 + n, part)[:, kt, :] for part in range(2)],
                                    [t[:, kt, :] for t in moving], first, last_)

                n0, banks, used = plan.at[f"up{layer}"]
                with pe.Fori(0, 4, 1) as i:
                    for j in range(BANKS):
                        pe.wait_ge(w_split, i * 8 + (split0 + j + 1))
                        pe.wait_ge(bank_free[banks[j]], i + used[j])
                        for kt in range(KT):
                            last = mlp_products(bank[banks[j]][:, 0:SEQ], j, [h[:, :, real] for h in h_hl], kt,
                                                kt == 0, kt == KT - 1)
                        last.then_inc(group_done, 1)
                n0, banks, used = plan.at[f"down{layer}"]
                pe.wait_ge(u_step, 3 * FF // P * (layer + 1))
                with pe.Fori(0, 2, 1) as i:
                    for half in range(2):
                        two = banks[2 * half:2 * half + 2]
                        for j in range(2):
                            pe.wait_ge(bank_free[two[j]], i + used[2 * half + j])
                        for q in range(4):
                            for j in range(2):
                                n = MLP_UNITS // 2 + 8 * half + 2 * q + j
                                pe.wait_ge(w_split, i * 16 + (split0 + n + 1))
                                u_q = [u_[:, q * KT:(q + 1) * KT, :] for u_ in u_hl]
                                for kt in range(KT):
                                    last = mlp_products(bank[two[j]][:, 0:SEQ], n, u_q, kt,
                                                        q == 0 and kt == 0, q == 3 and kt == KT - 1)
                                last.then_inc(group_done, 1)

            mlp(0)
            norm(2)
            project([f"rg{m}" for m in range(2 * KT)], "rg_in", h_real, ready=h_wait(2))
            pe.wait_ge(bd_loaded, 64)
            for m in range(KT):
                pe.wait_ge(xc_ready, m + 2)
                pb = open_bank(f"ri{m}")
                mm(pb[:, 0:SEQ], bd[:, 0, m, :], xc[:, m, :], start=True, stop=True)
                mm(pb[:, SEQ:2 * SEQ], bd[:, 1, m, :], xc[:, m, :], start=True, stop=True).then_inc(group_done, 1)
            project([f"rgo{m}" for m in range(KT)], "rg_o", m_all, ready=lambda kt: (y_split, kt // 4 + 1))
            mlp(1)
            norm(4)
            norm(5)
            project([f"zr{m}" for m in range(ZT)], "w_rwkv", h_all, ready=h_wait(5))

            def one(name, lhsT, rhs):
                pb = open_bank(name)
                mm(pb[:, 0:rhs.shape[-1]], lhsT, rhs, start=True, stop=True).then_inc(group_done, 1)

            pe.wait_ge(consts_built, 3)
            pe.wait_ge(kks_ready, 1)
            for m in range(RT):
                one(f"kks{m}", head_sum[:], Kh[:, m, :])
            pe.wait_ge(updown_loaded, 48)
            pe.wait_ge(lw_ready, 2)
            for m in range(RT):
                one(f"wp{m}", updown[0:64, m * P:(m + 1) * P], tlw[0:64])
            for m in range(RT):
                one(f"ap{m}", updown[64:128, m * P:(m + 1) * P], zf[64:128, 12, :])
            for m in range(RT):
                one(f"gp{m}", gup[:, m * P:(m + 1) * P], slg)
            project([f"{n}{m}" for n in ("val", "cg") for m in range(RT)], "w_conv", h_all)
            pe.wait_ge(rk_ready, 1)
            for m in range(RT):
                one(f"bon{m}", head_sum[:], Kh[:, m, CH:WT])
            pe.wait_ge(kb_ready, 1)
            for tt in range(3):
                n = CH if tt == 0 else P
                c0 = 0 if tt == 0 else CH + (tt - 1) * P
                for s_, src in enumerate((vZ, Kh, Bh)):
                    pb = open_bank(f"nat{s_}_{tt}")
                    for m in range(RT):
                        last = transposed(pb[0:n, m * P:(m + 1) * P], src[:, m, c0:c0 + n], P)
                    last.then_inc(group_done, 1)

            def head(t, h, c):
                return t[HD * (h % 2):HD * (h % 2 + 1), h // 2, CH * c:CH * (c + 1)]

            def chunks_of(tt):
                return [0] if tt == 0 else [2 * tt - 1, 2 * tt]

            for tt in range(3):
                for s_, (left, right) in enumerate(((aa, kk), (kk, aa), (kZ, kk), (kZ, rZ), (aa, rZ))[:5 if tt else 3]):
                    for par_ in range(2):
                        pb = open_bank(f"mat{s_}_{par_}_{tt}")
                        for half, c in enumerate(chunks_of(tt)):
                            for q in range(4):
                                last = mm(pb[CH * half:CH * (half + 1), CH * q:CH * (q + 1)],
                                          head(left, 2 * q + par_, c), head(right, 2 * q + par_, c),
                                          start=True, stop=True)
                        last.then_inc(group_done, 1)

            def per_chunk(name, left, right, tt):
                pb = open_bank(name)
                for half in range(len(chunks_of(tt))):
                    r_ = slice(CH * half, CH * (half + 1))
                    for h in range(RH):
                        last = mm(pb[r_, CH * h:CH * (h + 1)], left[r_, tt, h, :], right[r_, tt, h, :],
                                  start=True, stop=True)
                last.then_inc(group_done, 1)

            for lv in range(1, LEVELS):
                for tt in range(3):
                    pe.wait_ge(mt_ready, 3 * (lv - 1) + tt + 1)
                    per_chunk(f"Y{lv}_{tt}", MT, X, tt)
                for tt in range(3):
                    wait_out(pe, f"Y{lv}_{tt}")
                    if lv < LEVELS - 1:
                        per_chunk(f"XY{lv}_{tt}", XT, Y, tt)
                    per_chunk(f"YX{lv}_{tt}", Y, XT, tt)
            natv = nat[0].rearrange("p t (h v) -> p t h v", v=HD)
            wait_out(pe, *[f"mat2_{par_}_{tt}" for tt in range(3) for par_ in range(2)])
            for tt in range(3):
                per_chunk(f"GV_{tt}", G1, natv, tt)
            wait_out(pe, *[f"YX{LEVELS - 1}_{tt}" for tt in range(3)])
            for c in range(NCH):
                tt = (c + 1) // 2
                p0 = CH * ((c - 1) % 2) if c else 0
                r_ = slice(p0, p0 + CH)
                old = ST[:, c % 2]
                if c:
                    pe.wait_ge(st_ready, c)
                    for par_ in range(2):
                        pb = open_bank(f"SA{par_}_{c}")
                        for q in range(4):
                            last = mm(pb[r_, CH * q:CH * (q + 1)], head(kk, 2 * q + par_, c),
                                      old[HD * par_:HD * (par_ + 1), q, :], start=True, stop=True)
                        last.then_inc(group_done, 1)
                    pb = open_bank(f"OA_{c}")
                    for h in range(RH):
                        h_ = slice(HD * (h % 2), HD * (h % 2 + 1))
                        last = mm(pb[h_, CH * (h // 2):CH * (h // 2 + 1)], old[h_, h // 2, :], head(rZ, h, c),
                                  start=True, stop=True)
                    last.then_inc(group_done, 1)

                def block(pb, h):
                    return pb[HD * (h % 2):HD * (h % 2 + 1), CH * (h // 2):CH * (h // 2 + 1)]

                ps = open_bank(f"S_{c}")
                for h in range(RH):
                    hc = slice(HD * h, HD * (h + 1))
                    mm(block(ps, h), nat[1][r_, tt, hc], nat[0][r_, tt, hc], start=h < 2, stop=False,
                       skip_group_check=True)
                pb = open_bank(f"U_{c}")
                pe.wait_ge(yc_ready, c + 1)
                for h in range(RH):
                    last = mm(pb[r_, CH * h:CH * (h + 1)], XT[r_, tt, h, :], Yc[r_, h, :], start=True, stop=True)
                last.then_inc(group_done, 1)
                if c:
                    po = open_bank(f"OB_{c}")
                    for h in range(RH):
                        mm(block(po, h), nat[0][r_, tt, HD * h:HD * (h + 1)], G2[r_, tt - 1, h, :],
                           start=h < 2, stop=False, skip_group_check=True)
                wait_out(pe, f"U_{c}")
                for h in range(RH):
                    last = mm(block(ps, h), nat[2][r_, tt, HD * h:HD * (h + 1)], Uc[r_, h, :],
                              start=False, stop=h >= RH - 2, skip_group_check=True)
                last.then_inc(group_done, 1)
                if c:
                    for h in range(RH):
                        last = mm(block(po, h), Uc[r_, h, :], G3[r_, tt - 1, h, :], start=False,
                                  stop=h >= RH - 2, skip_group_check=True)
                    last.then_inc(group_done, 1)
            pe.wait_ge(owk_ready, 1)
            for m in range(RT):
                one(f"gm{m}", head_mean[:], owk[:, m, :])
            pe.wait_ge(osq_ready, 1)
            for m in range(RT):
                one(f"gv{m}", head_mean[:], osq[:, m, :])
            for name, src, ready in (("lm", cy, cy_ready), ("lv", ct, csq_ready)):
                pe.wait_ge(ready, 1)
                pb = open_bank(name)
                for m in range(RT):
                    last = mm(pb[:, 0:SEQ], mean_c[:], src[:, m, :], start=m == 0, stop=m == RT - 1)
                last.then_inc(group_done, 1)
                first = 0 if name == "lm" else KT
                project([f"gl{m}" for m in range(first, first + KT)], "w_gate", h_real, first=first)
            pe.wait_ge(y_split, 3)
            project([f"yb{m}" for m in range(KT)], "rwkv_out", lambda kt: [y[:, kt, :] for y in y_hl])
            pe.wait_ge(y_split, 4)
            project([f"ya{m}" for m in range(KT)], "conv_out", lambda kt: [y[:, RT + kt, :] for y in y_hl])
            project([f"wo2{m}" for m in range(KT)], "wo2", h_real, ready=lambda kt: (mix_split, kt + 1))
            norm(6)
            w = slot(SLOTS["keys"], NK)
            for m in range(4):
                pb = open_bank(f"key{m}")
                for j in range(4):
                    last = transposed(pb[:, j * P:(j + 1) * P], w[:, 4 * m + j, :], P)
                last.then_inc(group_done, 1)
            wait_out(pe, *[f"key{m}" for m in range(4)])

            def scores(tt, m):
                pb = open_bank(f"sc{tt}_{m}")
                wait_out(pe, *[f"pq{j}" for j in range(4 * m, 4 * m + 4)])
                for j in range(4):
                    last = mm(pb[:, j * P:(j + 1) * P], pq[:, 4 * m + j, tt * P:(tt + 1) * P],
                              keyT[:, 4 * m + j, :], start=True, stop=True)
                last.then_inc(group_done, 1)

            for m in range(5):
                if m < 4:
                    project([f"pq{j}" for j in range(4 * m, 4 * m + 4)], "w_q", h_real,
                            ready=h_wait(6) if m == 0 else None, first=4 * m)
                if m:
                    scores(0, m - 1)
            for tt in range(2):
                for name, src in (("xn", hT), ("hn", xT)):
                    for m in range(2):
                        pb = open_bank(f"{name}{tt}_{m}")
                        for j in range(4):
                            last = transposed(pb[:, j * P:(j + 1) * P],
                                              src[:, 4 * m + j, META + tt * P:META + (tt + 1) * P], P)
                        last.then_inc(group_done, 1)
            for m in range(4):
                scores(1, m)
            wait_out(pe, *[f"{name}1_{m}" for name in ("xn", "hn") for m in range(2)])
            n = len(PE_ROWS)
            for tt in range(2):
                for half in range(2):
                    mm(y_banks[tt][half][:, :], ident[:], hnat[:, tt, 512 * half:512 * (half + 1)],
                       start=True, stop=True)
                first = (2 * tt + 1) * (SEL // GR)
                with pe.Fori(0, SEL // GR, 1) as i:
                    for k, j in enumerate(PE_ROWS):
                        pe.wait_ge(diag_ready, i * n + (n * (SEL // GR) * tt + k + 1))
                        pe.wait_ge(row_loaded[j], i * 16 + 16 * (first + 1))
                        for half in range(2):
                            last = mm(y_banks[tt][half][:, :], diag[:, k, :], grow(j)[:, 512 * half:512 * (half + 1)],
                                      start=False, stop=True, skip_group_check=True)
                        last.then_inc(pe_used, 1)


_INS = ['x', 'norm_mix', 'norm_mlp', 'mlp_w1', 'mlp_w2', 'sb_w_qkv', 'sb_w_o', 'rg_w_in', 'rg_conv_w',
        'rg_conv_b', 'rg_w_a', 'rg_b_a', 'rg_w_x', 'rg_b_x', 'rg_lambda', 'rg_w_o', 'norm_final',
        'meta_tokens_2', 'g_mix_2', 'w_in_2', 'conv_w_2', 'conv_b_2', 'conv_ln_g_2', 'conv_ln_b_2',
        'w_conv_out_2', 'mu_shift_2', 'w0_2', 'w_up_2', 'a0_2', 'a_up_2', 'g_up_2', 'k_k_2', 'k_a_2',
        'r_k_2', 'gn_g_2', 'gn_b_2', 'w_rwkv_out_2', 'w_o_2', 'g_ffn_2', 'w_q_2', 'sub_keys_2',
        'expert_u_2', 'expert_v_2', 'g_final_2']


def kernel(**inputs):
    import numpy as _np
    import concourse.bacc as _bacc
    from concourse import mybir as _mybir
    from concourse.bass_utils import run_bass_kernel_spmd as _run

    nc = _bacc.Bacc("TRN2", target_bir_lowering=False, num_devices=1)
    arrays, args = {}, []
    for name in _INS:
        a = _np.ascontiguousarray(inputs[name])
        arrays[f"in_{name}_dram"] = a
        args.append(nc.dram_tensor(f"in_{name}_dram", a.shape, _mybir.dt.from_np(a.dtype), kind="ExternalInput").ap())
    shape = (1, SEQ, D)
    args.append(nc.dram_tensor("out_0_dram", shape, _mybir.dt.float32, kind="ExternalOutput").ap())
    build(nc, *args)
    r = _run(nc, [arrays], core_ids=[0])
    return r.results[0]["out_0_dram"]
```
